# Optimizing a Trainium2 kernel written in Bass

```python
import jax, jax.numpy as jnp
from jax import lax
import numpy as np

D_MODEL = 1024
BATCH = 1
SEQ = 512
DEPTH = 2

CHUNK = 64
Q_BLOCK = 128

ATT_HEADS = 8
ATT_HEAD_DIM = 64
ATT_WIDTH = ATT_HEADS * ATT_HEAD_DIM
IDX_HEADS = 8
IDX_HEAD_DIM = 64
TOPK_MAX = 256

POOL_GROUPS = 4
POOL_GROUP_DIM = 64
POOL_WIDTH = POOL_GROUPS * POOL_GROUP_DIM
POOL_WINDOWS = (2, 4, 8, 16)

CONV_WIDTH = 256
CONV_KERNEL = 31

MIX_WIDTH = ATT_WIDTH + POOL_WIDTH + CONV_WIDTH
IN_SIZES = (ATT_WIDTH, ATT_WIDTH, ATT_WIDTH,
            IDX_HEADS * IDX_HEAD_DIM, IDX_HEAD_DIM, IDX_HEADS,
            POOL_WIDTH,
            2 * CONV_WIDTH)
N_IN = sum(IN_SIZES)

N_GROUPS = 4
EXPERTS_PER_GROUP = 4
EXPERT_HIDDEN = 512
TOP_K_EXPERTS = 2

EPS = 1e-6

kernel_name = "hybrid_dsa_pool_conformer_hiermoe"

def rmsnorm(x, g):
    xf = x.astype(jnp.float32)
    y = xf * lax.rsqrt(jnp.mean(xf * xf, axis=-1, keepdims=True) + EPS)
    return (y * g.astype(jnp.float32)).astype(x.dtype)

def split_columns(p):
    offsets = []
    acc = 0
    for s in IN_SIZES[:-1]:
        acc += s
        offsets.append(acc)
    return jnp.split(p, offsets, axis=-1)

def dsa_attention(q, k, v, q_idx, k_idx, w_idx):
    B, S = q.shape[0], q.shape[1]
    nb = S // Q_BLOCK
    k_top = min(TOPK_MAX, S // 4)
    key_chunk = jnp.arange(S, dtype=jnp.int32) // CHUNK
    pos_blocks = jnp.arange(S, dtype=jnp.int32).reshape(nb, Q_BLOCK)
    k_idx_f = k_idx.astype(jnp.float32)
    att_scale = ATT_HEAD_DIM ** -0.5

    def to_blocks(a):
        return a.reshape((B, nb, Q_BLOCK) + a.shape[2:]).swapaxes(0, 1)

    def block_fn(args):
        qb, qib, wb, pos = args
        q_chunk = pos // CHUNK
        dots = jnp.einsum('bqhd,bsd->bqhs', qib.astype(jnp.float32), k_idx_f) * (IDX_HEAD_DIM ** -0.5)
        score = jnp.einsum('bqhs,bqh->bqs', jax.nn.relu(dots), wb.astype(jnp.float32)) * (IDX_HEADS ** -0.5)
        admissible = key_chunk[None, :] <= q_chunk[:, None]
        score = jnp.where(admissible[None], score, -jnp.inf)
        _, sel = lax.top_k(score, k_top)
        sel_ok = key_chunk[sel] <= q_chunk[None, :, None]
        k_sel = jax.vmap(lambda kb, ib: kb[ib])(k, sel)
        v_sel = jax.vmap(lambda vb, ib: vb[ib])(v, sel)
        logits = jnp.einsum('bqhd,bqkhd->bqhk', qb, k_sel).astype(jnp.float32) * att_scale
        logits = jnp.where(sel_ok[:, :, None, :], logits, -jnp.inf)
        p = jax.nn.softmax(logits, axis=-1).astype(v.dtype)
        return jnp.einsum('bqhk,bqkhd->bqhd', p, v_sel)

    out = lax.map(block_fn, (to_blocks(q), to_blocks(q_idx), to_blocks(w_idx), pos_blocks))
    return out.swapaxes(0, 1).reshape(B, S, ATT_HEADS * ATT_HEAD_DIM)

def pool_mixer(u, pool_w, pool_scale):
    B, S, _ = u.shape
    uf = u.astype(jnp.float32)
    csum = jnp.concatenate([jnp.zeros((B, 1, POOL_WIDTH), jnp.float32), jnp.cumsum(uf, axis=1)], axis=1)
    t1 = jnp.arange(1, S + 1, dtype=jnp.float32)
    pooled = []
    for gi, w in enumerate(POOL_WINDOWS):
        c = csum[..., gi * POOL_GROUP_DIM:(gi + 1) * POOL_GROUP_DIM]
        lagged = jnp.pad(c, ((0, 0), (w, 0), (0, 0)))[:, :S + 1]
        window_sum = c[:, 1:] - lagged[:, 1:]
        count = jnp.minimum(t1, jnp.float32(w))
        pooled.append(window_sum / count[None, :, None])
    d = (jnp.concatenate(pooled, axis=-1) - uf).astype(u.dtype)
    d = d.reshape(B, S, POOL_GROUPS, POOL_GROUP_DIM)
    y = jnp.einsum('bsgc,gcd->bsgd', d, pool_w).reshape(B, S, POOL_WIDTH)
    return y * pool_scale

def conformer_conv(u, dw_w, dw_b, ln_g, ln_b, pw_w, pw_b):
    a, gate = jnp.split(u, 2, axis=-1)
    h = a * jax.nn.sigmoid(gate)
    h = lax.conv_general_dilated(h, dw_w[:, None, :], window_strides=(1,),
                                 padding=[(CONV_KERNEL - 1, 0)],
                                 dimension_numbers=('NWC', 'WIO', 'NWC'),
                                 feature_group_count=CONV_WIDTH) + dw_b
    hf = h.astype(jnp.float32)
    mu = jnp.mean(hf, axis=-1, keepdims=True)
    var = jnp.mean(jnp.square(hf - mu), axis=-1, keepdims=True)
    hf = (hf - mu) * lax.rsqrt(var + EPS) * ln_g.astype(jnp.float32) + ln_b.astype(jnp.float32)
    h = jax.nn.silu(hf).astype(u.dtype)
    return h @ pw_w + pw_b

def hier_moe(h, rg_w, rg_b, re_w, re_b, w_gate, w_up, w_down):
    B, S, D = h.shape
    t = h.reshape(B * S, D)
    g_prob = jax.nn.softmax((t @ rg_w + rg_b).astype(jnp.float32), axis=-1)
    g_sel = jnp.argmax(g_prob, axis=-1)
    p_g = jnp.take_along_axis(g_prob, g_sel[:, None], axis=1)[:, 0]
    e_logits = (t @ re_w + re_b).astype(jnp.float32).reshape(-1, N_GROUPS, EXPERTS_PER_GROUP)
    e_in = jnp.take_along_axis(e_logits, g_sel[:, None, None], axis=1)[:, 0]
    e_prob = jax.nn.softmax(e_in, axis=-1)
    top_v, top_i = lax.top_k(e_prob, TOP_K_EXPERTS)
    top_v = top_v / jnp.sum(top_v, axis=-1, keepdims=True)
    w_e = jnp.sum(jax.nn.one_hot(top_i, EXPERTS_PER_GROUP, dtype=jnp.float32) * top_v[..., None], axis=1)
    gate = (jax.nn.one_hot(g_sel, N_GROUPS, dtype=jnp.float32)[:, :, None]
            * (p_g[:, None, None] * w_e[:, None, :])).astype(h.dtype)
    y = jnp.zeros_like(t)
    for gi in range(N_GROUPS):
        a = jnp.einsum('td,edh->teh', t, w_gate[gi])
        b = jnp.einsum('td,edh->teh', t, w_up[gi])
        act = jax.nn.silu(a) * b * gate[:, gi, :, None]
        y = y + jnp.einsum('teh,ehd->td', act, w_down[gi])
    return y.reshape(B, S, D)

def setup_inputs(seed: int = 0) -> dict:
    key = jax.random.key(seed)
    ks = jax.random.split(key, 24)
    f32 = jnp.float32
    n = lambda k, shape: jax.random.normal(k, shape, f32)
    L, D, G, E, H = DEPTH, D_MODEL, N_GROUPS, EXPERTS_PER_GROUP, EXPERT_HIDDEN
    return {
        "x": n(ks[0], (BATCH, SEQ, D)),
        "norm1_g": 1.0 + 0.02 * n(ks[1], (L, D)),
        "w_in": n(ks[2], (L, D, N_IN)) * D ** -0.5,
        "pool_w": n(ks[3], (L, POOL_GROUPS, POOL_GROUP_DIM, POOL_GROUP_DIM)) * POOL_GROUP_DIM ** -0.5,
        "pool_scale": 1.0 + 0.02 * n(ks[4], (L, POOL_WIDTH)),
        "dw_w": n(ks[5], (L, CONV_KERNEL, CONV_WIDTH)) * CONV_KERNEL ** -0.5,
        "dw_b": 0.02 * n(ks[6], (L, CONV_WIDTH)),
        "conv_ln_g": 1.0 + 0.02 * n(ks[7], (L, CONV_WIDTH)),
        "conv_ln_b": 0.02 * n(ks[8], (L, CONV_WIDTH)),
        "pw_w": n(ks[9], (L, CONV_WIDTH, CONV_WIDTH)) * CONV_WIDTH ** -0.5,
        "pw_b": 0.02 * n(ks[10], (L, CONV_WIDTH)),
        "w_out": n(ks[11], (L, MIX_WIDTH, D)) * MIX_WIDTH ** -0.5,
        "norm2_g": 1.0 + 0.02 * n(ks[12], (L, D)),
        "rg_w": n(ks[13], (L, D, G)) * D ** -0.5,
        "rg_b": 0.01 * n(ks[14], (L, G)),
        "re_w": n(ks[15], (L, D, G * E)) * D ** -0.5,
        "re_b": 0.01 * n(ks[16], (L, G * E)),
        "w_gate": n(ks[17], (L, G, E, D, H)) * D ** -0.5,
        "w_up": n(ks[18], (L, G, E, D, H)) * D ** -0.5,
        "w_down": n(ks[19], (L, G, E, H, D)) * H ** -0.5,
        "final_g": 1.0 + 0.02 * n(ks[20], (D,)),
    }

def reference(x, norm1_g, w_in, pool_w, pool_scale, dw_w, dw_b, conv_ln_g, conv_ln_b, pw_w, pw_b,
              w_out, norm2_g, rg_w, rg_b, re_w, re_b, w_gate, w_up, w_down, final_g):
    B, S, _ = x.shape
    for l in range(DEPTH):
        h = rmsnorm(x, norm1_g[l])
        proj = h @ w_in[l]
        q, k, v, qi, ki, wi, pool_in, conv_in = split_columns(proj)
        q = q.reshape(B, S, ATT_HEADS, ATT_HEAD_DIM)
        k = k.reshape(B, S, ATT_HEADS, ATT_HEAD_DIM)
        v = v.reshape(B, S, ATT_HEADS, ATT_HEAD_DIM)
        qi = qi.reshape(B, S, IDX_HEADS, IDX_HEAD_DIM)
        y_a = dsa_attention(q, k, v, qi, ki, wi)
        y_b = pool_mixer(pool_in, pool_w[l], pool_scale[l])
        y_c = conformer_conv(conv_in, dw_w[l], dw_b[l], conv_ln_g[l], conv_ln_b[l], pw_w[l], pw_b[l])
        x = x + jnp.concatenate([y_a, y_b, y_c], axis=-1) @ w_out[l]
        h2 = rmsnorm(x, norm2_g[l])
        x = x + hier_moe(h2, rg_w[l], rg_b[l], re_w[l], re_b[l], w_gate[l], w_up[l], w_down[l])
    return rmsnorm(x, final_g)


_drawn_inputs = setup_inputs


def setup_inputs(seed=0):
    import zlib

    import numpy as np

    out = dict(_drawn_inputs(seed))
    spreads = {}
    factors = {'re_b': 2.879, 'final_g': 2.957}
    for name, (base, spread) in spreads.items():
        noise = np.random.default_rng([zlib.crc32(name.encode()), seed]).standard_normal(out[name].shape)
        drawn = base * np.exp(spread * noise) if base else spread * noise
        out[name] = __import__('jax').numpy.asarray(drawn.astype(out[name].dtype))
    for name, factor in factors.items():
        out[name] = (out[name] * factor).astype(out[name].dtype)
    return out
```

```python
from contextlib import ExitStack

import numpy as np

import concourse.bass as bass
from concourse import mybir

F32 = mybir.dt.float32
F32R = mybir.dt.float32r
I32 = mybir.dt.int32
ALU = mybir.AluOpType
ACT = mybir.ActivationFunctionType
AX = mybir.AxisListType.X

P = 128
D = 1024
SEQ = 512
DEPTH = 2
TT = SEQ // P
DC = D // P
HEADS, HD = 8, 64
CHUNK = 64
TOPK = min(256, SEQ // 4)
ROUNDS = TOPK // 8
CW = 256
TAPS = 31
NG, NE, TOPE = 4, 4, 2
E = NG * NE
HID = 512
EPS = 1e-6
ATT_SCALE = float(HD) ** -0.5
IDX_SCALE = float(HD) ** -0.5 * float(HEADS) ** -0.5
NEG_INADM, NEG_TAKEN, NEG_TEST = -3.0e38, -3.4e38, -3.3e38
MASKED = -1.0e30

G_CONV, G_QI, G_KI, G_K, G_Q, G_V = range(6)
GROUPS = [(2376, 512), (1536, 512), (2048, 328), (512, 512), (0, 512), (1024, 512)]
PIECES_GROUP = 4
PIECES_IN = PIECES_GROUP * len(GROUPS)
PIECES_MIX = PIECES_IN + 8
PIECES_E = 12
PIECES_L = PIECES_MIX + E * PIECES_E
RAW = 12
SPL = 4
EXTRA = (TOPE * SEQ - E) // P
TILES = E + EXTRA
KEYS = [P * (b + 1) for b in range(TT)]
SC_AT = [None, 0, 256, 640]
SCORES = 1152
UNITS = TT * HEADS
VECS = TAPS + 5
V_DWB, V_LNG, V_LNB, V_PWB, V_PSC = range(TAPS, TAPS + 5)

C_ID, C_TRI, C_ONE = 0, 128, 256
C_E, C_REV, C_J, C_PW, C_PH = 384, 400, 404, 411, 413
C_N = C_PH + 32

A_HROW = 0
A_QT, A_KT = 0, 2048
A_V = 4096
A_KI = 6144
A_P = A_KI
A_HPAD = 7168
A_ACC = A_HPAD + 2 * 542
A_SQ = A_ACC + 1024
A_U = A_SQ + 1024
A_UT = A_U + 2 * 528
A_SC = A_UT + 2 * 528
A_MB0 = A_SC + SCORES
A_L = A_MB0 + 128
A_PT = A_L + 1024
A_O = A_PT + 1024
A_N = A_O + 512
A_Y = A_L


def trunk(nc, t, out):
    with ExitStack() as ctx:
        def sb(name, shape, dt=F32):
            return ctx.enter_context(nc.sbuf_tensor(name, shape, dt))

        def sem(name):
            return ctx.enter_context(nc.semaphore(name))

        arena = sb("arena", [P, A_N])
        x = sb("x_sb", [P, TT, D])
        a_hi = sb("a_hi", [P, DC, SEQ], F32R)
        a_lo = sb("a_lo", [P, DC, SEQ], F32R)
        raw = sb("raw", [P, RAW, 1024])
        w_hi = sb("w_hi", [P, SPL, 1024], F32R)
        w_lo = sb("w_lo", [P, SPL, 1024], F32R)
        gain = sb("gain", [P, D])
        cst = sb("cst", [P, C_N])
        pw = sb("pw", [P, 2, CW])
        pbd = sb("pbd", [P, DEPTH, 2, P])
        rw = sb("rw", [P, DEPTH, DC, 20])
        rw_hi = sb("rw_hi", [P, DEPTH, DC, 20], F32R)
        rw_lo = sb("rw_lo", [P, DEPTH, DC, 20], F32R)
        rb = sb("rb", [P, DEPTH, 20])
        chan = sb("chan", [P, DEPTH, 2, VECS])
        widx = sb("widx", [P, TT, HEADS])
        top8 = sb("top8", [P, 3, 8])
        stat = sb("stat", [P, 3, UNITS])
        rinv = sb("rinv", [P, HEADS])
        nrm = sb("nrm", [P, 4, TT])
        tok = sb("tok", [P, TT], I32)
        tab = sb("tab", [P, TILES], I32)
        zero = sb("zero", [P, TILES], I32)
        tidx = sb("tidx", [P, TT * TOPE], I32)
        yidx = sb("yidx", [P, TT * TOPE], I32)
        ovx = sb("ovx", [P, EXTRA + 1], I32)
        gates = sb("gates", [P, TT, TOPE])

        ps = ctx.enter_context(nc.psum_tensor("ps", [P, 8, 512], F32))

        h2d = [nc.dram_tensor(f"h2_rows{l}", (SEQ, D), F32, kind="Internal").ap() for l in range(DEPTH)]
        tabd = [nc.dram_tensor(f"tok_table{l}", (P * TILES, 1), I32, kind="Internal").ap() for l in range(DEPTH)]
        yd = nc.dram_tensor("y_rows", (TILES * P, D), F32, kind="Internal").ap()

        def ar(at, n, *dims):
            v = arena[:, at:at + n]
            if len(dims) == 2:
                return v.rearrange("p (a n) -> p a n", a=dims[0])
            return v

        hrow = ar(A_HROW, 4096, TT, D)
        qT, kT = ar(A_QT, 2048, 4, SEQ), ar(A_KT, 2048, 4, SEQ)
        qiT, v_sb = ar(A_V, 2048, 4, SEQ), ar(A_V, 2048, 4, SEQ)
        kiT, wT = ar(A_KI, 512), ar(A_KI + 512, 512)
        hpad = ar(A_HPAD, 1084, 2, 542)
        acc = ar(A_ACC, 1024, 2, SEQ)
        sq = ar(A_SQ, 1024, 2, SEQ)
        u = ar(A_U, 1056, 2, 528)
        ut = ar(A_UT, 1056, 2, 528)
        mask = [arena[:, A_MB0:A_MB0 + P]] + [arena[:, A_SC + SC_AT[b]:A_SC + SC_AT[b] + KEYS[b]] for b in range(1, TT)]
        lsb = ar(A_L, 1024, 2, 512)
        prob = ar(A_P, 1024, 2, 512)
        pT = ar(A_PT, 1024, 2, 512)
        osb = ar(A_O, 512)
        vrows = ar(A_PT, DEPTH * CW, DEPTH, CW)
        pl = ln_t = hpad[:, :, 30:542]
        xg = ar(A_V, D)
        slu, act = ar(A_V + 1024, HID), ar(A_V + 1536, HID)
        ysb = ar(A_Y, D)
        yc = ar(A_HROW, 4096, 4, D)
        ident = cst[:, C_ID:C_ID + P]
        ones = cst[:, C_ONE:C_ONE + P]
        tri = cst[:, C_TRI:C_TRI + P]

        at = A_SC
        R = {}
        for name, dims in (("lg", (20,)), ("gd", (4,)), ("ge", (4,)), ("fe", (4,)), ("ei", (4,)), ("t4", (4,)), ("og", (4,)),
                           ("o1", (4,)), ("o2", (4,)), ("t1", ()), ("f1", ()), ("f2", ()), ("gs", ()), ("pg", ()),
                           ("pr", (NG, NE)), ("m1", (NG, NE)), ("m2", (NG, NE)), ("ms", (NG, NE)), ("tm", (E,)),
                           ("p2", (2,)), ("b2", (2,)), ("e2", (2,)), ("k2", (2,)), ("v2", (2,))):
            n = TT * int(np.prod(dims))
            view = arena[:, at:at + n]
            if len(dims) == 1:
                view = view.rearrange("p (t n) -> p t n", t=TT)
            elif len(dims) == 2:
                view = view.rearrange("p (t g i) -> p t g i", t=TT, g=NG)
            R[name] = view
            at += n
        for name, n in (("cn", E), ("ex", E), ("cum", E), ("base", E), ("oe", EXTRA), ("cmp", EXTRA * E)):
            R[name] = arena[:, at:at + n]
            at += n
        R["cmp"] = R["cmp"].rearrange("p (j e) -> p j e", j=EXTRA)
        assert at <= A_SC + SCORES
        head = sb("head", [P, 2, 16])[:]

        par_in, x_in, pads, ids_set = sem("par_in"), sem("x_in"), sem("pads"), sem("ids_set")
        chan_t, chan_set, rw_split = sem("chan_t"), sem("chan_set"), sem("rw_split")
        dve_step, act_step = sem("dve_step"), sem("act_step")
        raw_in = [sem(f"raw_in{s}") for s in range(RAW)]
        w_hi_set, w_lo_set, w_used = sem("w_hi_set"), sem("w_lo_set"), sem("w_used")
        gain_in, ssq_set, ms_set, rms_set, hrow_set = (sem(n) for n in ("gain_in", "ssq_set", "ms_set", "rms_set", "hrow_set"))
        ht_ready, ht_hi, ht_lo = sem("ht_ready"), sem("ht_hi"), sem("ht_lo")
        proj_ready = sem("proj_ready")
        qi_set, ki_set, u_set, sig_set, glu_set, k_set, q_set, v_set = (
            sem(n) for n in ("qi_set", "ki_set", "u_set", "sig_set", "glu_set", "k_set", "q_set", "v_set"))
        wt_ready, widx_set, dots_ready, relu_set, idx_acc, inadm_set, topk_step = (
            sem(n) for n in ("wt_ready", "widx_set", "dots_ready", "relu_set", "idx_acc", "inadm_set", "topk_step"))
        conv_tap, pool_d, pw_in = sem("conv_tap"), sem("pool_d"), sem("pw_in")
        qk_ready, logit_set, negmax_set, exp_set, pt_ready, pt_set, pv_ready, o_set, ot_ready = (
            sem(n) for n in ("qk_ready", "logit_set", "negmax_set", "exp_set", "pt_ready", "pt_set", "pv_ready", "o_set", "ot_ready"))
        pool_ready, mean_ready, ln_d, ln_sq, var_ready, ln_ms, ln_rms, ln_n, ln_y, pw_ready = (
            sem(n) for n in ("pool_ready", "mean_ready", "ln_d", "ln_sq", "var_ready", "ln_ms", "ln_rms", "ln_n", "ln_y", "pw_ready"))
        o_hi_set, o_lo_set, pw_hi, pw_lo, pool_hi, pool_lo = (
            sem(n) for n in ("o_hi_set", "o_lo_set", "pw_hi", "pw_lo", "pool_hi", "pool_lo"))
        out_ready, x_mixed = sem("out_ready"), sem("x_mixed")
        rlog_ready, exp_in, exp_out, route_set, pos_ready, slots_set = (
            sem(n) for n in ("rlog_ready", "exp_in", "exp_out", "route_set", "pos_ready", "slots_set"))
        y_zero = sem("y_zero")
        h2_stored, tab_zero, tab_put, tab_in = sem("h2_stored"), sem("tab_zero"), sem("tab_put"), sem("tab_in")
        yc_in = [sem(f"yc_in{q}") for q in range(4)]
        x_moe, out_set, out_done = sem("x_moe"), sem("out_set"), sem("out_done")

        class Tiles:
            def __init__(self, tag, own_ring):
                self.xg_in = sem(f"xg_in{tag}")
                self.xt_ready = sem(f"xt_ready{tag}")
                self.xt_hi = sem(f"xt_hi{tag}")
                self.xt_lo = sem(f"xt_lo{tag}")
                self.silu_set = sem(f"silu_set{tag}")
                self.act_set = sem(f"act_set{tag}")
                self.at_ready = sem(f"at_ready{tag}")
                self.at_hi = sem(f"at_hi{tag}")
                self.at_lo = sem(f"at_lo{tag}")
                self.y_set_a = sem(f"y_set_a{tag}")
                self.y_set_v = sem(f"y_set_v{tag}")
                self.y_stored = sem(f"y_stored{tag}")
                self.slots = SPL if own_ring else RAW
                if own_ring:
                    self.raw_in = [sem(f"raw_in{s}{tag}") for s in range(SPL)]
                    self.w_hi_set, self.w_lo_set, self.w_used = sem(f"w_hi_set{tag}"), sem(f"w_lo_set{tag}"), sem(f"w_used{tag}")
                else:
                    self.raw_in, self.w_hi_set, self.w_lo_set, self.w_used = raw_in, w_hi_set, w_lo_set, w_used

        main = Tiles("", False)
        over = [Tiles(f"_over{l}", True) for l in range(DEPTH)]

        def cnt(i, per, c):
            return c if i is None else i * per + c

        def free_slot(sp, S, i, n):
            if i is not None or n >= S.slots:
                sp.wait_ge(S.w_lo_set, cnt(i, PIECES_E, n - S.slots + 1))

        def load(sp, S, n, halves):
            for dst, src in halves:
                sp.dma_start(dst, src).then_inc(S.raw_in[n % S.slots], 16)

        def load_in(sp, l, n, g, j):
            c0, w = GROUPS[g]
            free_slot(sp, main, None, n)
            load(sp, main, n, [(raw[:, n % RAW, a * w:(a + 1) * w],
                                t["w_in"][l, (2 * j + a) * P:(2 * j + a + 1) * P, c0:c0 + w]) for a in range(2)])

        def load_out(sp, l, n, j):
            free_slot(sp, main, None, n)
            load(sp, main, n, [(raw[:, n % RAW, a * 512:(a + 1) * 512],
                                t["w_out"][l, j * P:(j + 1) * P, a * 512:(a + 1) * 512]) for a in range(2)])

        def load_gu(sp, S, l, i, n, e, c):
            free_slot(sp, S, i, n)
            load(sp, S, n, [(raw[:, n % S.slots, a * 512:(a + 1) * 512],
                             t[w][bass.ds(e + l * E, 1), c * P:(c + 1) * P, :].rearrange("a p n -> (a p) n"))
                            for a, w in enumerate(("w_gate", "w_up"))])

        def load_down(sp, S, l, i, n, e, j):
            free_slot(sp, S, i, n)
            load(sp, S, n, [(raw[:, n % S.slots, a * 512:(a + 1) * 512],
                             t["w_down"][bass.ds(e + l * E, 1), j * P:(j + 1) * P, a * 512:(a + 1) * 512]
                             .rearrange("a p n -> (a p) n")) for a in range(2)])

        def hi(eng, S, i, n, w=1024):
            eng.wait_ge(S.raw_in[n % S.slots], cnt(i, 32, 32 * (n // S.slots + 1)))
            if i is not None or n >= SPL:
                eng.wait_ge(S.w_used, cnt(i, PIECES_E, n - SPL + 1))
            nc.scalar.activation(w_hi[:, n % SPL, 0:w], raw[:, n % S.slots, 0:w], ACT.Copy).then_inc(S.w_hi_set, 1)

        def lo(eng, S, i, n, w=1024):
            eng.wait_ge(S.w_hi_set, cnt(i, PIECES_E, n + 1))
            nc.vector.tensor_tensor(w_lo[:, n % SPL, 0:w], raw[:, n % S.slots, 0:w], w_hi[:, n % SPL, 0:w].bitcast(F32),
                                    ALU.subtract).then_inc(S.w_lo_set, 1)

        def use(pe, S, i, n):
            pe.wait_ge(S.w_lo_set, cnt(i, PIECES_E, n + 1))

        def three(o, lh, ll, rh, rl, start, stop):
            nc.tensor.matmul(o, lh, rh, start=start, stop=False)
            nc.tensor.matmul(o, lh, rl, start=False, stop=False)
            return nc.tensor.matmul(o, ll, rh, start=False, stop=stop)

        def bank_ready(eng, l, g, m):
            banks = 3 if g == G_KI else 4
            if m == banks - 1:
                eng.wait_ge(w_used, l * PIECES_L + (g + 1) * PIECES_GROUP)
            else:
                eng.wait_ge(proj_ready, 17 * l + 3 * g - (g > G_KI) + m + 1)

        block = ctx.enter_context(nc.Block())

        @block.sync
        def _(sp):
            for tt in range(TT):
                sp.dma_start(x[:, tt, :], t["x"][0, tt * P:(tt + 1) * P, :]).then_inc(x_in, 16)
            for l in range(DEPTH):
                n = l * PIECES_L
                for g in range(len(GROUPS)):
                    for j in range(PIECES_GROUP):
                        load_in(sp, l, n, g, j)
                        n += 1
                for j in range(8):
                    load_out(sp, l, n, j)
                    n += 1
                for c in range(8):
                    load_gu(sp, main, l, None, n + c, 0, c)
                n += 8

                def step(i):
                    for c in range(8):
                        load_gu(sp, main, l, i, n + c, cnt(i, 1, 1), c)
                    for j in range(4):
                        load_down(sp, main, l, i, n + 8 + j, cnt(i, 1, 0), j)

                step(None)
                with sp.Fori(1, E - 1) as i:
                    step(i)
                n += PIECES_E * (E - 1)
                for j in range(4):
                    load_down(sp, main, l, None, n + j, E - 1, j)
                n += 4
                sp.wait_ge(slots_set, l + 1)
                extra = sp.value_load(ovx[0:1, EXTRA:EXTRA + 1], min_val=0, max_val=EXTRA)
                with sp.If(extra > 0):
                    sp.wait_ge(main.w_lo_set, n)
                    for j in range(EXTRA):
                        e = sp.value_load(ovx[0:1, j:j + 1], min_val=0, max_val=E - 1)
                        for c in range(8):
                            load_gu(sp, over[l], l, None, j * PIECES_E + c, e, c)
                        for d in range(4):
                            load_down(sp, over[l], l, None, j * PIECES_E + 8 + d, e, d)
                    sp.wait_ge(over[l].w_lo_set, EXTRA * PIECES_E)
            for tt in range(TT):
                sp.wait_ge(out_set, tt + 1)
                sp.dma_start(out[0, tt * P:(tt + 1) * P, :], hrow[:, tt, :]).then_inc(out_done, 16)
            sp.wait_ge(out_done, 16 * TT)

        N_DMA = 9 + DEPTH * 4

        @block.gpsimd
        def _(pool):
            g = nc.gpsimd
            for v in (hpad[:, :, 0:30], u[:, :, 0:16], ut[:, :, 0:16], pbd[:]):
                g.memset(v, 0.0).then_inc(pads, 1)
            g.memset(mask[0], 0.0).then_inc(pads, 1)
            pool.wait_ge(pads, 5)
            g.memset(arena[0:CHUNK, A_MB0 + CHUNK:A_MB0 + P], MASKED).then_inc(pads, 1)
            g.memset(zero[:], 0).then_inc(pads, 1)
            g.memset(acc, 0.0).then_inc(pads, 1)
            g.iota(tok[:], pattern=[[P, TT]], base=0, channel_multiplier=1).then_inc(ids_set, 1)

            def gain_load(k):
                src = t["final_g"] if k == 2 * DEPTH else t["norm2_g" if k % 2 else "norm1_g"][k // 2]
                pool.dma_start(gain[:], src.partition_broadcast(P)).then_inc(gain_in, 16)

            gain_load(0)
            pool.dma_start(cst[:], t["shape_constants"]).then_inc(par_in, 16)
            pool.dma_start(rb[:, :, 0:NG], t["rg_b"].partition_broadcast(P)).then_inc(par_in, 16)
            pool.dma_start(rb[:, :, NG:20], t["re_b"].partition_broadcast(P)).then_inc(par_in, 16)
            pool.dma_start(vrows[0:TAPS], t["dw_w"].rearrange("l k c -> k l c")).then_inc(par_in, 16)
            for row, name in ((V_DWB, "dw_b"), (V_LNG, "conv_ln_g"), (V_LNB, "conv_ln_b"), (V_PWB, "pw_b"), (V_PSC, "pool_scale")):
                pool.dma_start(vrows[row:row + 1], t[name].unsqueeze(0)).then_inc(par_in, 16)
            for l in range(DEPTH):
                pool.dma_start(rw[:, l, :, 0:NG], t["rg_w"][l].rearrange("(c p) n -> p c n", p=P),
                               allow_slow_non_contiguous=True).then_inc(par_in, 16)
                pool.dma_start(rw[:, l, :, NG:20], t["re_w"][l].rearrange("(c p) n -> p c n", p=P),
                               allow_slow_non_contiguous=True).then_inc(par_in, 16)
                for h in range(2):
                    pool.dma_start(pbd[h * 64:(h + 1) * 64, l, :, h * 64:(h + 1) * 64],
                                   t["pool_w"][l, h::2].rearrange("g c d -> c g d")).then_inc(par_in, 16)
            pool.wait_ge(pads, 8)
            for l in range(DEPTH):
                pool.dma_start(tabd[l].rearrange("(p a) b -> p (a b)", a=TILES), zero[:]).then_inc(tab_zero, 16)
            for j in range(EXTRA):
                pool.dma_start(yd[(E + j) * P:(E + j + 1) * P, :], acc.rearrange("p a n -> p (a n)")).then_inc(y_zero, 16)

            for l in range(DEPTH):
                if l:
                    pool.wait_ge(pw_ready, 2 * l)
                pool.dma_start(pw[:], t["pw_w"][l].rearrange("(c p) n -> p c n", p=P)).then_inc(pw_in, 16)
                k = 2 * l + 1
                pool.wait_ge(hrow_set, 4 * k)
                gain_load(k)
                for tt in range(TT):
                    pool.wait_ge(hrow_set, 4 * k + tt + 1)
                    pool.dma_start(h2d[l][tt * P:(tt + 1) * P, :], hrow[:, tt, :]).then_inc(h2_stored, 16)
                gain_load(k + 1)
                pool.wait_ge(slots_set, l + 1)
                if l == 0:
                    pool.wait_ge(tab_zero, 16 * DEPTH)
                    pool.wait_ge(ids_set, 1)
                for q in range(TT * TOPE):
                    pool.indirect_dma_start(tabd[l], bass.IndirectOffsetOnAxis(ap=tidx[:, q:q + 1], axis=0),
                                            tok[:, q // TOPE:q // TOPE + 1], None).then_inc(tab_put, 16)
                pool.wait_ge(tab_put, 16 * TT * TOPE * (l + 1))
                if l:
                    pool.wait_ge(main.xg_in, 16 * (E + 1) * l)
                pool.dma_start(tab[:], tabd[l].rearrange("(p a) b -> p (a b)", a=TILES)).then_inc(tab_in, 16)
                pool.wait_ge(tab_in, 16 * (l + 1))
                pool.wait_ge(h2_stored, 16 * TT * (l + 1))

                def gather(S, col, i, c):
                    if i is not None or c > 0:
                        pool.wait_ge(S.xt_ready, cnt(i, 2, 2 * c))
                    pool.indirect_dma_start(xg, None, h2d[l], bass.IndirectOffsetOnAxis(ap=tab[:, col:col + 1], axis=0)
                                            ).then_inc(S.xg_in, 16)

                def store(S, tile, i, c):
                    pool.wait_ge(S.y_set_a, cnt(i, 1, c))
                    pool.wait_ge(S.y_set_v, cnt(i, 1, c))
                    pool.dma_start(yd[tile * P:(tile + 1) * P, :], ysb).then_inc(S.y_stored, 16)

                for e in range(E + 1):
                    gather(main, e, None, (E + 1) * l + e)
                    if e >= 3:
                        store(main, e - 3, None, E * l + e - 2)
                for e in range(E - 2, E):
                    store(main, e, None, E * l + e + 1)
                extra = pool.value_load(ovx[0:1, EXTRA:EXTRA + 1], min_val=0, max_val=EXTRA)
                with pool.If(extra > 0):
                    pool.wait_ge(y_zero, 16 * EXTRA)
                    pool.wait_ge(main.xt_ready, 2 * (E + 1) * (l + 1))
                    for j in range(EXTRA):
                        gather(over[l], E + j, None, j)
                        store(over[l], E + j, None, j + 1)
                    pool.wait_ge(over[l].y_stored, 16 * EXTRA)
                if l == 0:
                    pool.wait_ge(y_zero, 16 * EXTRA)
                pool.wait_ge(main.y_stored, 16 * E * (l + 1))
                for tt in range(TT):
                    if tt >= 2:
                        pool.wait_ge(x_moe, 2 * TT * l + 2 * (tt - 1))
                    for k2 in range(TOPE):
                        q = TOPE * tt + k2
                        pool.indirect_dma_start(yc[:, q % 4, :], None, yd,
                                                bass.IndirectOffsetOnAxis(ap=yidx[:, q:q + 1], axis=0)
                                                ).then_inc(yc_in[q % 4], 16)

        @block.tensor
        def _(pe):
            T = nc.tensor

            def norm_transposes(k):
                pe.wait_ge(hrow_set, 4 * (k + 1))
                for c in range(DC):
                    for tt in range(TT):
                        mm = T.transpose(ps[:, c, tt * P:(tt + 1) * P], hrow[:, tt, c * P:(c + 1) * P], ident)
                    mm.then_inc(ht_ready, 1)

            def project(l, g, banks):
                w = GROUPS[g][1]
                cols = [(0, 72), (72, P), (200, P)] if g == G_KI else [(m * P, P) for m in range(4)]
                n = l * PIECES_L + g * PIECES_GROUP
                for j in range(PIECES_GROUP):
                    use(pe, main, None, n + j)
                    if g == G_CONV:
                        pe.wait_ge(ht_lo, 16 * l + 8)
                    for a in range(2):
                        c = 2 * j + a
                        s = (n + j) % SPL
                        for m, (c0, M) in enumerate(cols):
                            if g == G_V:
                                tk = slice(m * P, (m + 1) * P)
                                mm = three(ps[:, banks[m], :], a_hi[:, c, tk], a_lo[:, c, tk],
                                           w_hi[:, s, a * w:(a + 1) * w], w_lo[:, s, a * w:(a + 1) * w], c == 0, c == DC - 1)
                            else:
                                k0 = a * w + c0
                                mm = three(ps[0:M, banks[m], :], w_hi[:, s, k0:k0 + M], w_lo[:, s, k0:k0 + M],
                                           a_hi[:, c, :], a_lo[:, c, :], c == 0, c == DC - 1)
                            if j == PIECES_GROUP - 1 and a == 1 and m < len(cols) - 1:
                                mm.then_inc(proj_ready, 1)
                    mm.then_inc(w_used, 1)

            def router(l):
                pe.wait_ge(ht_lo, 16 * l + 16)
                for tt in range(TT):
                    for c in range(DC):
                        tk = slice(tt * P, (tt + 1) * P)
                        mm = three(ps[:, 0, tt * 32:tt * 32 + 20], a_hi[:, c, tk], a_lo[:, c, tk],
                                   rw_hi[:, l, c, :], rw_lo[:, l, c, :], c == 0, c == DC - 1)
                mm.then_inc(rlog_ready, 1)
                pe.wait_ge(route_set, l + 1)
                m_sel = R["ms"].rearrange("p t g i -> p t (g i)")
                for tt in range(TT):
                    for s in range(tt + 1):
                        T.matmul(ps[:, 1, tt * E:(tt + 1) * E], tri if s == tt else ones, m_sel[:, s, :],
                                 start=(s == 0), stop=(s == tt))
                for s in range(TT):
                    mm = T.matmul(ps[:, 1, TT * E:(TT + 1) * E], ones, m_sel[:, s, :], start=(s == 0), stop=(s == TT - 1))
                mm.then_inc(pos_ready, 1)

            def tile_rows(S, i, c):
                pe.wait_ge(S.xg_in, cnt(i, 16, 16 * (c + 1)))
                if i is not None or c:
                    pe.wait_ge(S.xt_lo, cnt(i, 2, 2 * c))
                for h in range(2):
                    for q in range(4):
                        mm = T.transpose(ps[:, 2 + h, q * P:(q + 1) * P], xg[:, (4 * h + q) * P:(4 * h + q + 1) * P], ident)
                    mm.then_inc(S.xt_ready, 1)

            def tile_gu(S, i, c, n, xc):
                pe.wait_ge(S.xt_lo, cnt(i, 2, 2 * (xc + 1)))
                if i is not None or c:
                    pe.wait_ge(S.act_set, cnt(i, 1, c))
                for k in range(8):
                    use(pe, S, i, n + k)
                    s = (n + k) % SPL
                    for h in range(2):
                        mm = three(ps[:, h, :], a_hi[:, k, 0:P], a_lo[:, k, 0:P],
                                   w_hi[:, s, h * 512:(h + 1) * 512], w_lo[:, s, h * 512:(h + 1) * 512], k == 0, k == 7)
                    mm.then_inc(S.w_used, 1)

            def tile_act(S, i, c):
                pe.wait_ge(S.act_set, cnt(i, 1, c + 1))
                for q in range(4):
                    mm = T.transpose(ps[:, 4, q * P:(q + 1) * P], act[:, q * P:(q + 1) * P], ident)
                mm.then_inc(S.at_ready, 1)

            def tile_down(S, i, c, n):
                pe.wait_ge(S.at_lo, cnt(i, 1, c + 1))
                if i is not None or c:
                    pe.wait_ge(S.y_set_a, cnt(i, 1, c))
                    pe.wait_ge(S.y_set_v, cnt(i, 1, c))
                for k in range(4):
                    use(pe, S, i, n + k)
                    s = (n + k) % SPL
                    for h in range(2):
                        mm = three(ps[:, 5 + h, :], a_hi[:, k, P:2 * P], a_lo[:, k, P:2 * P],
                                   w_hi[:, s, h * 512:(h + 1) * 512], w_lo[:, s, h * 512:(h + 1) * 512], k == 0, k == 3)
                    mm.then_inc(S.w_used, 1)

            pe.wait_ge(par_in, 16 * N_DMA)
            for l in range(DEPTH):
                for h in range(2):
                    mm = T.transpose(ps[:, 7, (2 * l + h) * VECS:(2 * l + h + 1) * VECS],
                                     vrows[0:VECS, l, h * P:(h + 1) * P], cst[0:VECS, C_ID:C_ID + VECS])
            mm.then_inc(chan_t, 1)
            pe.wait_ge(chan_set, 1)

            for l in range(DEPTH):
                if l:
                    pe.wait_ge(x_moe, 2 * TT * l)
                norm_transposes(2 * l)
                project(l, G_CONV, [4, 5, 6, 7])
                project(l, G_QI, [0, 1, 2, 3])
                pe.wait_ge(glu_set, 2 * (l + 1))
                project(l, G_KI, [4, 5, 6])
                pe.wait_ge(ki_set, 3 * (l + 1))
                for tt in range(TT):
                    mm = T.transpose(ps[:, 7, tt * HEADS:(tt + 1) * HEADS], wT[64:72, tt * P:(tt + 1) * P],
                                     cst[64:72, C_ID + 64:C_ID + 72])
                mm.then_inc(wt_ready, 1)
                pe.wait_ge(qi_set, 4 * (l + 1))
                for v in range(24):
                    h, b = v // 3, v % 3 + 1
                    r = slice((h % 2) * 64, (h % 2) * 64 + 64)
                    if v >= 4:
                        pe.wait_ge(relu_set, 24 * l + v - 3)
                    T.matmul(ps[:, v % 4, 0:KEYS[b]], qiT[r, h // 2, b * P:(b + 1) * P], kiT[r, 0:KEYS[b]],
                             start=True, stop=True).then_inc(dots_ready, 1)
                pe.wait_ge(u_set, 2 * (l + 1))
                pe.wait_ge(widx_set, l + 1)
                project(l, G_K, [4, 5, 6, 7])
                pe.wait_ge(relu_set, 24 * (l + 1))
                project(l, G_Q, [0, 1, 2, 3])
                pe.wait_ge(k_set, 4 * (l + 1))
                project(l, G_V, [4, 5, 6, 7])

                pe.wait_ge(q_set, 4 * (l + 1))

                def turn_o(b):
                    pe.wait_ge(o_set, TT * l + b + 1)
                    if b:
                        pe.wait_ge(o_lo_set, TT * l + b)
                    for j in range(4):
                        mm = T.transpose(ps[:, 6, j * P:(j + 1) * P], osb[:, j * P:(j + 1) * P], ident)
                    mm.then_inc(ot_ready, 1)

                def other(s):
                    if s == 6:
                        pe.wait_ge(conv_tap, 2 * TAPS * (l + 1))
                        for m in range(2):
                            mm = T.matmul(ps[:, 7, :], ones, acc[:, m, :], start=(m == 0), stop=(m == 1))
                        mm.then_inc(mean_ready, 1)
                    if s == 10:
                        pe.wait_ge(ln_sq, 2 * (l + 1))
                        for m in range(2):
                            mm = T.matmul(ps[:, 7, :], ones, sq[:, m, :], start=(m == 0), stop=(m == 1))
                        mm.then_inc(var_ready, 1)
                    if s in (17, 20):
                        m = (17, 20).index(s)
                        if m == 0:
                            pe.wait_ge(ln_y, 2 * (l + 1))
                            pe.wait_ge(pw_in, 16 * (l + 1))
                        else:
                            pe.wait_ge(pw_lo, 2 * l + 1)
                        for c in range(2):
                            mm = T.matmul(ps[:, 7, :], pw[:, c, m * P:(m + 1) * P], sq[:, c, :], start=(c == 0), stop=(c == 1))
                        mm.then_inc(pw_ready, 1)
                    if s in (27, 30):
                        m = (27, 30).index(s)
                        if m == 0:
                            pe.wait_ge(pw_lo, 2 * (l + 1))
                            pe.wait_ge(pool_d, l + 1)
                        else:
                            pe.wait_ge(pool_lo, 2 * l + 1)
                        T.matmul(ps[:, 7, :], pbd[:, l, m, :], ut[:, m, 16:528], start=True, stop=True).then_inc(pool_ready, 1)

                for s in range(UNITS + 2):
                    if s < UNITS:
                        b, h = s // HEADS, s % HEADS
                        r = slice((h % 2) * 64, (h % 2) * 64 + 64)
                        if s >= 2:
                            pe.wait_ge(logit_set, UNITS * l + s - 1)
                        T.matmul(ps[:, s % 2, 0:KEYS[b]], qT[r, h // 2, b * P:(b + 1) * P], kT[r, h // 2, 0:KEYS[b]],
                                 start=True, stop=True).then_inc(qk_ready, 1)
                    if 1 <= s <= UNITS:
                        w = s - 1
                        pe.wait_ge(exp_set, UNITS * l + w + 1)
                        if w >= 2:
                            pe.wait_ge(pt_set, UNITS * l + w - 1)
                        for kb in range(w // HEADS + 1):
                            mm = T.transpose(ps[:, 2 + w % 2, kb * P:(kb + 1) * P], prob[:, w % 2, kb * P:(kb + 1) * P], ident)
                        mm.then_inc(pt_ready, 1)
                    other(s)
                    if s >= 2:
                        w = s - 2
                        b, h = w // HEADS, w % HEADS
                        if w == 0:
                            pe.wait_ge(v_set, 4 * (l + 1))
                        pe.wait_ge(pt_set, UNITS * l + w + 1)
                        if h == 0 and b >= 2:
                            pe.wait_ge(o_set, TT * l + b - 1)
                        for kb in range(b + 1):
                            mm = T.matmul(ps[:, 4 + b % 2, h * HD:(h + 1) * HD], pT[:, w % 2, kb * P:(kb + 1) * P],
                                          v_sb[:, kb, h * HD:(h + 1) * HD], start=(kb == 0), stop=(kb == b))
                        mm.then_inc(pv_ready, 1)
                    if s >= 11 and (s - 11) % HEADS == 0:
                        turn_o((s - 11) // HEADS)
                turn_o(TT - 1)
                pe.wait_ge(pool_lo, 2 * (l + 1))
                pe.wait_ge(o_lo_set, TT * (l + 1))
                n = l * PIECES_L + PIECES_IN
                for j in range(8):
                    use(pe, main, None, n + j)
                    s = (n + j) % SPL
                    for tt in range(TT):
                        for h in range(2):
                            tk = slice(tt * P, (tt + 1) * P)
                            mm = three(ps[:, 2 * tt + h, :], a_hi[:, j, tk], a_lo[:, j, tk],
                                       w_hi[:, s, h * 512:(h + 1) * 512], w_lo[:, s, h * 512:(h + 1) * 512], j == 0, j == 7)
                            if j == 7 and 2 * tt + h < 7:
                                mm.then_inc(out_ready, 1)
                    mm.then_inc(w_used, 1)

                pe.wait_ge(x_mixed, 8 * (l + 1))
                norm_transposes(2 * l + 1)
                router(l)
                pe.wait_ge(slots_set, l + 1)
                n = l * PIECES_L + PIECES_MIX
                te, tx = E * l, (E + 1) * l
                tile_rows(main, None, tx)
                tile_gu(main, None, te, n, tx)
                tile_rows(main, None, tx + 1)
                tile_act(main, None, te)
                n += 8

                def step(i):
                    tile_gu(main, i, te + 1, n, tx + 1)
                    tile_rows(main, i, tx + 2)
                    tile_down(main, i, te, n + 8)
                    tile_act(main, i, te + 1)

                step(None)
                with pe.Fori(1, E - 1) as i:
                    step(i)
                tile_down(main, None, te + E - 1, n + PIECES_E * (E - 1))
                extra = pe.value_load(ovx[0:1, EXTRA:EXTRA + 1], min_val=0, max_val=EXTRA)
                with pe.If(extra > 0):
                    pe.wait_ge(main.xt_lo, 2 * (tx + E + 1))
                    pe.wait_ge(main.y_set_a, te + E)
                    pe.wait_ge(main.y_set_v, te + E)
                    for j in range(EXTRA):
                        tile_rows(over[l], None, j)
                        tile_gu(over[l], None, j, j * PIECES_E, j)
                        tile_act(over[l], None, j)
                        tile_down(over[l], None, j, j * PIECES_E + 8)

        @block.scalar
        def _(sc):
            A = nc.scalar

            def norm_act(k, waits):
                for s, v in waits:
                    sc.wait_ge(s, v)
                for tt in range(TT):
                    A.activation(hrow[:, tt, :], x[:, tt, :], ACT.Square, accum_out=nrm[:, 0, tt:tt + 1]).then_inc(ssq_set, 1)
                sc.wait_ge(ms_set, k + 1)
                A.activation(nrm[:, 2, :], nrm[:, 1, :], ACT.Sqrt).then_inc(rms_set, 1)

            def norm_hi(k):
                for c in range(DC):
                    sc.wait_ge(ht_ready, DC * k + c + 1)
                    A.activation(a_hi[:, c, :], ps[:, c, :], ACT.Copy).then_inc(ht_hi, 1)

            def tile_xt(S, i, c):
                for h in range(2):
                    sc.wait_ge(S.xt_ready, cnt(i, 2, 2 * c + h + 1))
                    A.activation(a_hi[:, 4 * h:4 * h + 4, 0:P], ps[:, 2 + h, :].rearrange("p (q n) -> p q n", q=4),
                                 ACT.Copy).then_inc(S.xt_hi, 1)

            def tile_silu(S, i, n):
                sc.wait_ge(S.w_used, cnt(i, PIECES_E, n + 8))
                A.activation(slu, ps[:, 0, :], ACT.Silu).then_inc(S.silu_set, 1)

            def tile_at(S, i, c):
                sc.wait_ge(S.at_ready, cnt(i, 1, c + 1))
                A.activation(a_hi[:, 0:4, P:2 * P], ps[:, 4, :].rearrange("p (q n) -> p q n", q=4),
                             ACT.Copy).then_inc(S.at_hi, 1)

            def tile_y(S, i, c, n):
                sc.wait_ge(S.w_used, cnt(i, PIECES_E, n + 4))
                if i is not None or c:
                    sc.wait_ge(S.y_stored, cnt(i, 16, 16 * c))
                A.activation(ysb[:, 0:512], ps[:, 5, :], ACT.Copy).then_inc(S.y_set_a, 1)

            for l in range(DEPTH):
                n0 = l * PIECES_L
                norm_act(2 * l, [(x_in, 16 * TT)] if l == 0 else [(x_moe, 2 * TT * l)])
                if l == 0:
                    for j in range(4):
                        hi(sc, main, None, j)
                norm_hi(2 * l)
                if l:
                    for j in range(4):
                        hi(sc, main, None, n0 + j)
                for j in range(4, 8):
                    hi(sc, main, None, n0 + j)
                for m in range(2):
                    bank_ready(sc, l, G_CONV, 2 + m)
                    A.activation(lsb[:, m, :], ps[:, 6 + m, :], ACT.Sigmoid).then_inc(sig_set, 1)
                for j in range(8, 12):
                    hi(sc, main, None, n0 + j, 2 * GROUPS[G_KI][1])
                for m in range(4):
                    bank_ready(sc, l, G_QI, m)
                    A.copy(qiT[:, m, :], ps[:, m, :]).then_inc(qi_set, 1)
                bank_ready(sc, l, G_KI, 0)
                A.copy(kiT[0:64, :], ps[0:64, 4, :]).then_inc(ki_set, 1)
                A.copy(kiT[64:128, :], ps[0:64, 4, :]).then_inc(ki_set, 1)
                A.copy(wT[64:72, :], ps[64:72, 4, :]).then_inc(ki_set, 1)
                for m in range(2):
                    bank_ready(sc, l, G_KI, 1 + m)
                    A.copy(u[:, m, 16:528], ps[:, 5 + m, :]).then_inc(u_set, 1)
                sc.wait_ge(wt_ready, l + 1)
                A.activation(widx[:].rearrange("p t h -> p (t h)"), ps[:, 7, 0:TT * HEADS], ACT.Copy,
                             scale=IDX_SCALE).then_inc(widx_set, 1)
                sc.wait_ge(glu_set, 2 * (l + 1))
                for v in range(24):
                    b = v % 3 + 1
                    sc.wait_ge(dots_ready, 24 * l + v + 1)
                    if v >= 2:
                        sc.wait_ge(idx_acc, 24 * l + v - 1)
                    A.activation(lsb[:, v % 2, 0:KEYS[b]], ps[:, v % 4, 0:KEYS[b]], ACT.Relu).then_inc(relu_set, 1)
                    if v % 6 == 5:
                        hi(sc, main, None, n0 + 12 + v // 6)
                for j in range(16, 20):
                    hi(sc, main, None, n0 + j)
                for m in range(4):
                    bank_ready(sc, l, G_K, m)
                    A.copy(kT[:, m, :], ps[:, 4 + m, :]).then_inc(k_set, 1)
                for j in range(20, 24):
                    hi(sc, main, None, n0 + j)
                for m in range(4):
                    bank_ready(sc, l, G_Q, m)
                    A.copy(qT[:, m, :], ps[:, m, :]).then_inc(q_set, 1)

                def o_hi(b):
                    sc.wait_ge(ot_ready, TT * l + b + 1)
                    A.activation(a_hi[:, 0:4, b * P:(b + 1) * P], ps[:, 6, :].rearrange("p (q n) -> p q n", q=4),
                                 ACT.Copy).then_inc(o_hi_set, 1)

                def other(s):
                    if s == 1:
                        for j in range(4):
                            hi(sc, main, None, n0 + PIECES_IN + j)
                    if s == 8:
                        for m in range(2):
                            sc.wait_ge(ln_d, 2 * l + m + 1)
                            A.activation(sq[:, m, :], acc[:, m, :], ACT.Square).then_inc(ln_sq, 1)
                    if s == 12:
                        sc.wait_ge(ln_ms, l + 1)
                        A.activation(ln_t[:, 1, :], ln_t[:, 0, :], ACT.Sqrt).then_inc(ln_rms, 1)
                    if s == 15:
                        for m in range(2):
                            sc.wait_ge(ln_n, 2 * l + m + 1)
                            A.activation(sq[:, m, :], acc[:, m, :], ACT.Silu, scale=chan[:, l, m, V_LNG:V_LNG + 1],
                                         bias=chan[:, l, m, V_LNB:V_LNB + 1]).then_inc(ln_y, 1)
                    if s in (18, 21):
                        m = (18, 21).index(s)
                        sc.wait_ge(pw_ready, 2 * l + m + 1)
                        A.activation(a_hi[:, 6 + m, :], ps[:, 7, :], ACT.Identity,
                                     bias=chan[:, l, m, V_PWB:V_PWB + 1]).then_inc(pw_hi, 1)
                    if s in (28, 31):
                        m = (28, 31).index(s)
                        sc.wait_ge(pool_ready, 2 * l + m + 1)
                        A.activation(a_hi[:, 4 + m, :], ps[:, 7, :], ACT.Copy,
                                     scale=chan[:, l, m, V_PSC:V_PSC + 1]).then_inc(pool_hi, 1)

                for s in range(UNITS + 1):
                    if s < UNITS:
                        K = KEYS[s // HEADS]
                        sc.wait_ge(negmax_set, UNITS * l + s + 1)
                        if s >= 2:
                            sc.wait_ge(pt_ready, UNITS * l + s - 1)
                        A.activation(prob[:, s % 2, 0:K], lsb[:, s % 2, 0:K], ACT.Exp, bias=stat[:, 1, s:s + 1],
                                     scale=ATT_SCALE, accum_out=stat[:, 2, s:s + 1]).then_inc(exp_set, 1)
                    if s == 0:
                        for m in range(4):
                            bank_ready(sc, l, G_V, m)
                            A.copy(v_sb[:, m, :], ps[:, 4 + m, :]).then_inc(v_set, 1)
                    if s >= 1:
                        w = s - 1
                        K = KEYS[w // HEADS]
                        sc.wait_ge(pt_ready, UNITS * l + w + 1)
                        if w >= 2:
                            sc.wait_ge(pv_ready, UNITS * l + w - 1)
                        A.copy(pT[:, w % 2, 0:K], ps[:, 2 + w % 2, 0:K]).then_inc(pt_set, 1)
                    other(s)
                    if s >= 12 and (s - 12) % HEADS == 0:
                        o_hi((s - 12) // HEADS)
                o_hi(TT - 1)
                for j in range(4, 12):
                    hi(sc, main, None, n0 + PIECES_IN + j)
                norm_act(2 * l + 1, [(x_mixed, 8 * (l + 1))])
                norm_hi(2 * l + 1)
                for q in range(2):
                    sc.wait_ge(exp_in, 2 * l + q + 1)
                    A.activation((R["ge"], R["fe"])[q], R["gd"], ACT.Exp).then_inc(exp_out, 1)
                sc.wait_ge(slots_set, l + 1)
                n = n0 + PIECES_MIX
                te, tx = E * l, (E + 1) * l
                tile_xt(main, None, tx)
                for k in range(4, 8):
                    hi(sc, main, None, n + k)
                tile_silu(main, None, n)
                tile_xt(main, None, tx + 1)
                for k in range(8, 12):
                    hi(sc, main, None, n + k)
                tile_at(main, None, te)
                n += 8

                def step(i):
                    for k in range(4, 12):
                        hi(sc, main, i, n + k)
                    tile_silu(main, i, n)
                    tile_xt(main, i, tx + 2)
                    for k in range(12, 16):
                        hi(sc, main, i, n + k)
                    tile_at(main, i, te + 1)
                    tile_y(main, i, te, n + 8)

                step(None)
                with sc.Fori(1, E - 1) as i:
                    step(i)
                tile_y(main, None, te + E - 1, n + PIECES_E * (E - 1))
                extra = sc.value_load(ovx[0:1, EXTRA:EXTRA + 1], min_val=0, max_val=EXTRA)
                with sc.If(extra > 0):
                    sc.wait_ge(main.w_used, (l + 1) * PIECES_L)
                    sc.wait_ge(main.y_stored, 16 * E * (l + 1))
                    for j in range(EXTRA):
                        O = over[l]
                        tile_xt(O, None, j)
                        for k in range(8):
                            hi(sc, O, None, PIECES_E * j + k)
                        tile_silu(O, None, PIECES_E * j)
                        tile_at(O, None, j)
                        for k in range(8, 12):
                            hi(sc, O, None, PIECES_E * j + k)
                        tile_y(O, None, j, PIECES_E * j + 8)
                    sc.wait_ge(over[l].w_used, EXTRA * PIECES_E)
            norm_act(2 * DEPTH, [(x_moe, 2 * TT * DEPTH)])

        @block.vector
        def _(ve):
            V = nc.vector
            steps = [0]

            def link(ins):
                steps[0] += 1
                ins.then_inc(dve_step, 1)
                ve.wait_ge(dve_step, steps[0])

            def norm_rows(k, waits):
                ve.wait_ge(ssq_set, TT * (k + 1))
                V.tensor_scalar(nrm[:, 1, :], nrm[:, 0, :], 1.0 / D, EPS, ALU.mult, ALU.add).then_inc(ms_set, 1)
                ve.wait_ge(rms_set, k + 1)
                link(V.reciprocal(nrm[:, 3, :], nrm[:, 2, :]))
                ve.wait_ge(gain_in, 16 * (k + 1))
                for tt in range(TT):
                    V.scalar_tensor_tensor(out=hrow[:, tt, :], in0=x[:, tt, :], scalar=nrm[:, 3, tt:tt + 1], in1=gain[:],
                                           op0=ALU.mult, op1=ALU.mult).then_inc(hrow_set, 1)

            def norm_lo(k):
                for c in range(DC):
                    ve.wait_ge(ht_hi, DC * k + c + 1)
                    V.tensor_tensor(a_lo[:, c, :], ps[:, c, :], a_hi[:, c, :].bitcast(F32), ALU.subtract).then_inc(ht_lo, 1)

            def topk_round(l, r):
                for b in range(1, TT):
                    s = 6 * r + b - 1
                    if s >= 3:
                        ve.wait_ge(topk_step, 99 * l + s - 2)
                    V.max(top8[:, b - 1, :], mask[b]).then_inc(topk_step, 1)
                for b in range(1, TT):
                    ve.wait_ge(topk_step, 99 * l + 6 * r + 3 + b - 1 - 2)
                    V.match_replace(mask[b], top8[:, b - 1, :], mask[b], NEG_TAKEN).then_inc(topk_step, 1)

            def conv(l, k):
                for m in range(2):
                    src, w = hpad[:, m, k:k + SEQ], chan[:, l, m, k:k + 1]
                    if k == 0:
                        ve.wait_ge(y_zero, 16 * EXTRA)
                        V.tensor_scalar(acc[:, m, :], src, w, chan[:, l, m, V_DWB:V_DWB + 1], ALU.mult, ALU.add
                                        ).then_inc(conv_tap, 1)
                    else:
                        ve.wait_ge(conv_tap, 2 * TAPS * l + 2 * k + m - 1)
                        V.scalar_tensor_tensor(out=acc[:, m, :], in0=src, scalar=w, in1=acc[:, m, :],
                                               op0=ALU.mult, op1=ALU.add).then_inc(conv_tap, 1)

            def pooling(l, part):
                table = cst[:, C_PH:C_PH + 32].rearrange("p (m n) -> p m n", m=2)
                if part == 0:
                    ve.wait_ge(u_set, 2 * (l + 1))
                    link(V.tensor_tensor(ut[:, :, 16:528], u[:, :, 16:528], u[:, :, 15:527], ALU.add))
                if part == 1:
                    link(V.tensor_tensor(pl, ut[:, :, 16:528], ut[:, :, 14:526], ALU.add))
                if part == 2:
                    V.tensor_copy(ut[:, 1, 16:20], pl[:, 1, 0:4])
                    link(V.tensor_tensor(ut[:, 1, 20:528], pl[:, 1, 4:512], pl[:, 1, 0:508], ALU.add))
                if part == 3:
                    link(V.tensor_tensor(pl[64:128, 1, :], ut[64:128, 1, 16:528], ut[64:128, 1, 8:520], ALU.add))
                    V.tensor_tensor(head[0:64], ut[0:64, :, 16:32], table[0:64], ALU.mult)
                    link(V.tensor_tensor(head[64:128], pl[64:128, :, 0:16], table[64:128], ALU.mult))
                if part in (4, 5):
                    m = part - 4
                    for r, s in ((slice(0, 64), ut[0:64, m, 16:528]), (slice(64, 128), pl[64:128, m, :])):
                        ins = V.scalar_tensor_tensor(out=ut[r, m, 16:528], in0=s, scalar=cst[r, C_PW + m:C_PW + m + 1],
                                                     in1=u[r, m, 16:528], op0=ALU.mult, op1=ALU.subtract)
                    link(ins)
                if part == 6:
                    V.tensor_tensor(ut[:, :, 16:32], head, u[:, :, 16:32], ALU.subtract).then_inc(pool_d, 1)

            def route(l):
                def b4(a, n):
                    return a.unsqueeze(2).to_broadcast([P, TT, n])

                ve.wait_ge(rlog_ready, l + 1)
                rev = cst[:, C_REV:C_REV + 4].unsqueeze(1).to_broadcast([P, TT, 4])
                link(V.tensor_tensor(R["lg"], ps[:, 0, 0:P].rearrange("p (t n) -> p t n", t=TT)[:, :, 0:20],
                                     rb[:, l, :].unsqueeze(1).to_broadcast([P, TT, 20]), ALU.add))

                def first_max(src, mx, hot):
                    link(V.tensor_reduce(mx, src, AX, ALU.max))
                    link(V.tensor_tensor(R["t4"], src, b4(mx, 4), ALU.is_ge))
                    link(V.tensor_tensor(R["t4"], R["t4"], rev, ALU.mult))
                    link(V.tensor_reduce(R["t1"], R["t4"], AX, ALU.max))
                    link(V.tensor_tensor(hot, rev, b4(R["t1"], 4), ALU.is_equal))

                link(V.tensor_reduce(R["t1"], R["lg"][:, :, 0:NG], AX, ALU.max))
                V.tensor_tensor(R["gd"], R["lg"][:, :, 0:NG], b4(R["t1"], NG), ALU.subtract).then_inc(exp_in, 1)
                ve.wait_ge(exp_out, 2 * l + 1)
                link(V.tensor_reduce(R["gs"], R["ge"], AX, ALU.add))
                first_max(R["ge"], R["f1"], R["og"])
                link(V.reciprocal(R["gs"], R["gs"]))
                link(V.tensor_tensor(R["pg"], R["f1"], R["gs"], ALU.mult))
                og4 = R["og"].unsqueeze(3).to_broadcast([P, TT, NG, NE])
                link(V.tensor_tensor(R["pr"], R["lg"][:, :, NG:20].rearrange("p t (g i) -> p t g i", g=NG), og4, ALU.mult))
                link(V.tensor_reduce(R["ei"], R["pr"].rearrange("p t g i -> p t i g"), AX, ALU.add))
                link(V.tensor_reduce(R["t1"], R["ei"], AX, ALU.max))
                V.tensor_tensor(R["gd"], R["ei"], b4(R["t1"], NE), ALU.subtract).then_inc(exp_in, 1)
                ve.wait_ge(exp_out, 2 * l + 2)
                first_max(R["fe"], R["f1"], R["o1"])
                link(V.scalar_tensor_tensor(out=R["fe"], in0=R["o1"], scalar=-2.0, in1=R["fe"], op0=ALU.mult, op1=ALU.add))
                first_max(R["fe"], R["f2"], R["o2"])
                link(V.tensor_tensor(R["t1"], R["f1"], R["f2"], ALU.add))
                link(V.reciprocal(R["t1"], R["t1"]))
                link(V.tensor_tensor(R["t1"], R["t1"], R["pg"], ALU.mult))
                V.tensor_tensor(gates[:, :, 0], R["f1"], R["t1"], ALU.mult)
                V.tensor_tensor(gates[:, :, 1], R["f2"], R["t1"], ALU.mult)
                V.tensor_tensor(R["m1"], og4, R["o1"].unsqueeze(2).to_broadcast([P, TT, NG, NE]), ALU.mult)
                link(V.tensor_tensor(R["m2"], og4, R["o2"].unsqueeze(2).to_broadcast([P, TT, NG, NE]), ALU.mult))
                V.tensor_tensor(R["ms"], R["m1"], R["m2"], ALU.add).then_inc(route_set, 1)
                ve.wait_ge(pos_ready, l + 1)
                link(V.tensor_copy(R["cn"], ps[:, 1, TT * E:(TT + 1) * E]))
                link(V.tensor_scalar(R["ex"], R["cn"], 128.0, None, ALU.is_gt))
                for q in (256.0, 384.0):
                    link(V.scalar_tensor_tensor(out=R["ex"], in0=R["cn"], scalar=q, in1=R["ex"], op0=ALU.is_gt, op1=ALU.add))
                link(V.tensor_tensor_scan(R["cum"], cst[:, C_ONE:C_ONE + E], R["ex"], 0.0, ALU.mult, ALU.add))
                V.tensor_copy(ovx[:, EXTRA:EXTRA + 1], R["cum"][:, E - 1:E])
                link(V.tensor_tensor(R["base"], R["cum"], R["ex"], ALU.subtract))
                link(V.tensor_tensor(R["cmp"], R["cum"].unsqueeze(1).to_broadcast([P, EXTRA, E]),
                                     cst[:, C_J:C_J + EXTRA].unsqueeze(2).to_broadcast([P, EXTRA, E]), ALU.is_le))
                link(V.tensor_reduce(R["oe"], R["cmp"], AX, ALU.add))
                link(V.tensor_scalar(ovx[:, 0:EXTRA], R["oe"], float(E - 1), None, ALU.min))
                for k, m in enumerate((R["m1"], R["m2"])):
                    m = m.rearrange("p t g i -> p t (g i)")
                    for dst, src in ((R["p2"], ps[:, 1, 0:TT * E].rearrange("p (t e) -> p t e", t=TT)),
                                     (R["b2"], R["base"].unsqueeze(1).to_broadcast([P, TT, E])),
                                     (R["e2"], cst[:, C_E:C_E + E].unsqueeze(1).to_broadcast([P, TT, E]))):
                        link(V.tensor_tensor(R["tm"], src, m, ALU.mult))
                        link(V.tensor_reduce(dst[:, :, k], R["tm"], AX, ALU.add))
                link(V.tensor_scalar(R["k2"], R["p2"], 128.0, None, ALU.is_ge))
                V.tensor_scalar(R["v2"], R["p2"], 128.0, None, ALU.is_ge)
                for q in (256.0, 384.0):
                    link(V.scalar_tensor_tensor(out=R["k2"], in0=R["p2"], scalar=q, in1=R["k2"], op0=ALU.is_ge, op1=ALU.add))
                link(V.scalar_tensor_tensor(out=R["p2"], in0=R["k2"], scalar=-128.0, in1=R["p2"], op0=ALU.mult, op1=ALU.add))
                link(V.tensor_tensor(R["b2"], R["b2"], R["k2"], ALU.add))
                link(V.tensor_tensor(R["b2"], R["b2"], R["e2"], ALU.subtract))
                link(V.scalar_tensor_tensor(out=R["b2"], in0=R["b2"], scalar=float(E - 1), in1=R["v2"], op0=ALU.add, op1=ALU.mult))
                link(V.tensor_tensor(R["e2"], R["e2"], R["b2"], ALU.add))
                t2 = tidx[:].rearrange("p (t k) -> p t k", k=TOPE)
                y2 = yidx[:].rearrange("p (t k) -> p t k", k=TOPE)
                V.scalar_tensor_tensor(out=t2, in0=R["p2"], scalar=float(TILES), in1=R["e2"], op0=ALU.mult, op1=ALU.add)
                link(V.scalar_tensor_tensor(out=y2, in0=R["e2"], scalar=float(P), in1=R["p2"], op0=ALU.mult, op1=ALU.add))
                V.engine_nop().then_inc(slots_set, 1)

            def tile_xt(S, i, c):
                for h in range(2):
                    ve.wait_ge(S.xt_hi, cnt(i, 2, 2 * c + h + 1))
                    V.tensor_tensor(a_lo[:, 4 * h:4 * h + 4, 0:P], ps[:, 2 + h, :].rearrange("p (q n) -> p q n", q=4),
                                    a_hi[:, 4 * h:4 * h + 4, 0:P].bitcast(F32), ALU.subtract).then_inc(S.xt_lo, 1)

            def tile_mul(S, i, c):
                ve.wait_ge(S.silu_set, cnt(i, 1, c + 1))
                V.tensor_tensor(act, ps[:, 1, :], slu, ALU.mult).then_inc(S.act_set, 1)

            def tile_at(S, i, c):
                ve.wait_ge(S.at_hi, cnt(i, 1, c + 1))
                V.tensor_tensor(a_lo[:, 0:4, P:2 * P], ps[:, 4, :].rearrange("p (q n) -> p q n", q=4),
                                a_hi[:, 0:4, P:2 * P].bitcast(F32), ALU.subtract).then_inc(S.at_lo, 1)

            def tile_y(S, i, c, n):
                ve.wait_ge(S.w_used, cnt(i, PIECES_E, n + 4))
                if i is not None or c:
                    ve.wait_ge(S.y_stored, cnt(i, 16, 16 * c))
                V.tensor_copy(ysb[:, 512:1024], ps[:, 6, :]).then_inc(S.y_set_v, 1)

            ve.wait_ge(par_in, 16 * N_DMA)
            V.tensor_copy(rw_hi[:], rw[:]).then_inc(rw_split, 1)
            ve.wait_ge(chan_t, 1)
            V.tensor_copy(chan[:].rearrange("p l h v -> p (l h v)"), ps[:, 7, 0:4 * VECS]).then_inc(chan_set, 1)
            ve.wait_ge(rw_split, 1)
            V.tensor_tensor(rw_lo[:], rw[:], rw_hi[:].bitcast(F32), ALU.subtract).then_inc(rw_split, 1)
            ve.wait_ge(chan_set, 1)
            ve.wait_ge(pads, 8)

            for l in range(DEPTH):
                n0 = l * PIECES_L
                norm_rows(2 * l, [])
                for j in range(4):
                    lo(ve, main, None, n0 + j)
                norm_lo(2 * l)
                for j in range(4, 8):
                    lo(ve, main, None, n0 + j)
                for m in range(2):
                    ve.wait_ge(sig_set, 2 * l + m + 1)
                    V.tensor_tensor(hpad[:, m, 30:542], ps[:, 4 + m, :], lsb[:, m, :], ALU.mult).then_inc(glu_set, 1)
                ve.wait_ge(glu_set, 2 * (l + 1))
                tap = 0
                for j in range(8, 12):
                    for k in range(3):
                        conv(l, tap)
                        tap += 1
                    lo(ve, main, None, n0 + j, 2 * GROUPS[G_KI][1])
                for k in range(8):
                    conv(l, tap)
                    tap += 1
                ve.wait_ge(widx_set, l + 1)
                for v in range(24):
                    h, b = v // 3, v % 3 + 1
                    ve.wait_ge(relu_set, 24 * l + v + 1)
                    src, w = lsb[:, v % 2, 0:KEYS[b]], widx[:, b, h:h + 1]
                    if h == 0:
                        V.tensor_scalar(mask[b], src, w, None, ALU.mult).then_inc(idx_acc, 1)
                    else:
                        ve.wait_ge(idx_acc, 24 * l + v - 2)
                        V.scalar_tensor_tensor(out=mask[b], in0=src, scalar=w, in1=mask[b],
                                               op0=ALU.mult, op1=ALU.add).then_inc(idx_acc, 1)
                    if v % 6 == 5:
                        lo(ve, main, None, n0 + 12 + v // 6)
                ve.wait_ge(idx_acc, 24 * (l + 1))
                for b in range(1, TT):
                    V.memset(mask[b][0:CHUNK, KEYS[b] - CHUNK:KEYS[b]], NEG_INADM).then_inc(inadm_set, 1)
                ve.wait_ge(inadm_set, 3 * (l + 1))
                for r in range(ROUNDS):
                    if r < 12 and r % 3 != 2:
                        lo(ve, main, None, n0 + 16 + r // 3 * 2 + r % 3)
                    topk_round(l, r)
                    if r >= 11:
                        conv(l, tap)
                        tap += 1
                for b in range(1, TT):
                    ve.wait_ge(topk_step, 99 * l + 96 - 2 + b - 1)
                    V.tensor_scalar(mask[b], mask[b], NEG_TEST, MASKED, ALU.is_gt, ALU.mult).then_inc(topk_step, 1)

                def o_lo(b):
                    ve.wait_ge(o_hi_set, TT * l + b + 1)
                    V.tensor_tensor(a_lo[:, 0:4, b * P:(b + 1) * P], ps[:, 6, :].rearrange("p (q n) -> p q n", q=4),
                                    a_hi[:, 0:4, b * P:(b + 1) * P].bitcast(F32), ALU.subtract).then_inc(o_lo_set, 1)

                def o_rows(b):
                    ve.wait_ge(pv_ready, UNITS * l + 8 * b + 8)
                    link(V.reciprocal(rinv[:], stat[:, 2, 8 * b:8 * b + 8]))
                    if b:
                        ve.wait_ge(ot_ready, TT * l + b)
                    V.tensor_tensor(osb.rearrange("p (h d) -> p h d", h=HEADS), ps[:, 4 + b % 2, :].rearrange("p (h d) -> p h d", h=HEADS),
                                    rinv[:].unsqueeze(2).to_broadcast([P, HEADS, HD]), ALU.mult).then_inc(o_set, 1)

                def other(s):
                    if s == 1:
                        for j in range(4):
                            lo(ve, main, None, n0 + PIECES_IN + j)
                    if s == 7:
                        ve.wait_ge(mean_ready, l + 1)
                        for m in range(2):
                            V.scalar_tensor_tensor(out=acc[:, m, :], in0=ps[:, 7, :], scalar=-1.0 / CW, in1=acc[:, m, :],
                                                   op0=ALU.mult, op1=ALU.add).then_inc(ln_d, 1)
                    if s == 11:
                        ve.wait_ge(var_ready, l + 1)
                        V.tensor_scalar(ln_t[:, 0, :], ps[:, 7, :], 1.0 / CW, EPS, ALU.mult, ALU.add).then_inc(ln_ms, 1)
                    if s == 13:
                        ve.wait_ge(ln_rms, l + 1)
                        V.reciprocal(ln_t[:, 0, 0:256], ln_t[:, 1, 0:256])
                    if s == 14:
                        link(V.reciprocal(ln_t[:, 0, 256:512], ln_t[:, 1, 256:512]))
                        for m in range(2):
                            V.tensor_tensor(acc[:, m, :], acc[:, m, :], ln_t[:, 0, :], ALU.mult).then_inc(ln_n, 1)
                    if s in (19, 22):
                        m = (19, 22).index(s)
                        ve.wait_ge(pw_hi, 2 * l + m + 1)
                        V.scalar_tensor_tensor(out=a_lo[:, 6 + m, :], in0=ps[:, 7, :], scalar=chan[:, l, m, V_PWB:V_PWB + 1],
                                               in1=a_hi[:, 6 + m, :].bitcast(F32), op0=ALU.add, op1=ALU.subtract).then_inc(pw_lo, 1)
                    if s in (29, 32):
                        m = (29, 32).index(s)
                        ve.wait_ge(pool_hi, 2 * l + m + 1)
                        V.scalar_tensor_tensor(out=a_lo[:, 4 + m, :], in0=ps[:, 7, :], scalar=chan[:, l, m, V_PSC:V_PSC + 1],
                                               in1=a_hi[:, 4 + m, :].bitcast(F32), op0=ALU.mult, op1=ALU.subtract).then_inc(pool_lo, 1)

                for s in range(UNITS):
                    b = s // HEADS
                    if s == HEADS:
                        ve.wait_ge(topk_step, 99 * (l + 1))
                    ve.wait_ge(qk_ready, UNITS * l + s + 1)
                    if s >= 2:
                        ve.wait_ge(exp_set, UNITS * l + s - 1)
                    V.tensor_tensor_reduce(lsb[:, s % 2, 0:KEYS[b]], ps[:, s % 2, 0:KEYS[b]], mask[b], 1.0, -3.0e38,
                                           ALU.add, ALU.max, stat[:, 0, s:s + 1]).then_inc(logit_set, 1)
                    ve.wait_ge(logit_set, UNITS * l + s + 1)
                    V.tensor_scalar(stat[:, 1, s:s + 1], stat[:, 0, s:s + 1], -ATT_SCALE, None, ALU.mult).then_inc(negmax_set, 1)
                    while tap < TAPS and s >= 1:
                        conv(l, tap)
                        tap += 1
                        if tap % 2:
                            break
                    if s >= 10 and (s - 10) % HEADS == 0:
                        o_rows((s - 10) // HEADS)
                    if s >= 13 and (s - 13) % HEADS == 0:
                        o_lo((s - 13) // HEADS)
                    other(s)
                    if 15 <= s < 25 and s not in (19, 22):
                        pooling(l, s - 15 - (s > 19) - (s > 22))
                o_rows(TT - 1)
                other(UNITS)
                o_lo(TT - 1)
                for j in range(4, 12):
                    lo(ve, main, None, n0 + PIECES_IN + j)
                for tt in range(TT):
                    for h in range(2):
                        if 2 * tt + h < 7:
                            ve.wait_ge(out_ready, 7 * l + 2 * tt + h + 1)
                        else:
                            ve.wait_ge(w_used, n0 + PIECES_MIX)
                        xs = x[:, tt, h * 512:(h + 1) * 512]
                        V.tensor_tensor(xs, ps[:, 2 * tt + h, :], xs, ALU.add).then_inc(x_mixed, 1)
                ve.wait_ge(x_mixed, 8 * (l + 1))
                norm_rows(2 * l + 1, [])
                norm_lo(2 * l + 1)
                route(l)
                n = n0 + PIECES_MIX
                te, tx = E * l, (E + 1) * l
                tile_xt(main, None, tx)
                for k in range(4, 8):
                    lo(ve, main, None, n + k)
                tile_mul(main, None, te)
                tile_xt(main, None, tx + 1)
                for k in range(8, 12):
                    lo(ve, main, None, n + k)
                tile_at(main, None, te)
                n += 8

                def step(i):
                    for k in range(4, 12):
                        lo(ve, main, i, n + k)
                    tile_mul(main, i, te + 1)
                    tile_xt(main, i, tx + 2)
                    for k in range(12, 16):
                        lo(ve, main, i, n + k)
                    tile_at(main, i, te + 1)
                    tile_y(main, i, te, n + 8)

                step(None)
                with ve.Fori(1, E - 1) as i:
                    step(i)
                tile_y(main, None, te + E - 1, n + PIECES_E * (E - 1))
                extra = ve.value_load(ovx[0:1, EXTRA:EXTRA + 1], min_val=0, max_val=EXTRA)
                with ve.If(extra > 0):
                    ve.wait_ge(main.w_used, (l + 1) * PIECES_L)
                    ve.wait_ge(main.y_stored, 16 * E * (l + 1))
                    for j in range(EXTRA):
                        O = over[l]
                        tile_xt(O, None, j)
                        for k in range(8):
                            lo(ve, O, None, PIECES_E * j + k)
                        tile_mul(O, None, j)
                        tile_at(O, None, j)
                        for k in range(8, 12):
                            lo(ve, O, None, PIECES_E * j + k)
                        tile_y(O, None, j, PIECES_E * j + 8)
                for tt in range(TT):
                    for k in range(TOPE):
                        q = TOPE * tt + k
                        ve.wait_ge(yc_in[q % 4], 16 * (2 * l + q // 4 + 1))
                        if k:
                            ve.wait_ge(x_moe, 2 * TT * l + q)
                        V.scalar_tensor_tensor(out=x[:, tt, :], in0=yc[:, q % 4, :], scalar=gates[:, tt, k:k + 1],
                                               in1=x[:, tt, :], op0=ALU.mult, op1=ALU.add).then_inc(x_moe, 1)
                ve.wait_ge(x_moe, 2 * TT * (l + 1))
            k = 2 * DEPTH
            ve.wait_ge(ssq_set, TT * (k + 1))
            V.tensor_scalar(nrm[:, 1, :], nrm[:, 0, :], 1.0 / D, EPS, ALU.mult, ALU.add).then_inc(ms_set, 1)
            ve.wait_ge(rms_set, k + 1)
            link(V.reciprocal(nrm[:, 3, :], nrm[:, 2, :]))
            ve.wait_ge(gain_in, 16 * (k + 1))
            for tt in range(TT):
                V.scalar_tensor_tensor(out=hrow[:, tt, :], in0=x[:, tt, :], scalar=nrm[:, 3, tt:tt + 1], in1=gain[:],
                                       op0=ALU.mult, op1=ALU.mult).then_inc(out_set, 1)


_INS = ["x", "norm1_g", "w_in", "pool_w", "pool_scale", "dw_w", "dw_b", "conv_ln_g", "conv_ln_b", "pw_w", "pw_b",
        "w_out", "norm2_g", "rg_w", "rg_b", "re_w", "re_b", "w_gate", "w_up", "w_down", "final_g"]


def shape_constants():
    c = np.zeros((P, C_N), np.float32)
    c[:, C_ID:C_ID + P] = np.eye(P)
    c[:, C_TRI:C_TRI + P] = np.triu(np.ones((P, P)), 1)
    c[:, C_ONE:C_ONE + P] = 1.0
    c[:, C_E:C_E + E] = np.arange(E)
    c[:, C_REV:C_REV + 4] = [4, 3, 2, 1]
    c[:, C_J:C_J + EXTRA] = np.arange(EXTRA)
    for m, r, w in ((0, 0, 2), (0, 1, 4), (1, 0, 8), (1, 1, 16)):
        rows = slice(64 * r, 64 * r + 64)
        c[rows, C_PW + m] = 1.0 / w
        c[rows, C_PH + 16 * m:C_PH + 16 * m + 16] = 1.0 / np.minimum(np.arange(1, 17), w)
    return c


def kernel(**inputs):
    import concourse.bacc as _bacc
    from concourse.bass_utils import run_bass_kernel_spmd as _run

    nc = _bacc.Bacc("TRN2", target_bir_lowering=False, num_devices=1)
    arrays, t = {}, {}
    for name in _INS + ["shape_constants"]:
        a = np.ascontiguousarray(shape_constants() if name == "shape_constants" else inputs[name])
        arrays[f"in_{name}"] = a
        t[name] = nc.dram_tensor(f"in_{name}", a.shape, mybir.dt.from_np(a.dtype), kind="ExternalInput").ap()
    for name in ("w_gate", "w_up", "w_down"):
        t[name] = t[name].rearrange("l g e a b -> (l g e) a b")
    out = nc.dram_tensor("out_0", (1, SEQ, D), F32, kind="ExternalOutput").ap()
    trunk(nc, t, out)
    r = _run(nc, [arrays], core_ids=[0])
    return r.results[0]["out_0"]
```

```python
from contextlib import ExitStack

import numpy as np

import concourse.bass as bass
from concourse import mybir

F32 = mybir.dt.float32
F32R = mybir.dt.float32r
I32 = mybir.dt.int32
ALU = mybir.AluOpType
ACT = mybir.ActivationFunctionType
AX = mybir.AxisListType.X

P = 128
D = 1024
SEQ = 512
DEPTH = 2
TT = SEQ // P
DC = D // P
HEADS, HD = 8, 64
CHUNK = 64
TOPK = min(256, SEQ // 4)
ROUNDS = TOPK // 8
CW = 256
TAPS = 31
NG, NE, TOPE = 4, 4, 2
E = NG * NE
HID = 512
EPS = 1e-6
ATT_SCALE = float(HD) ** -0.5
IDX_SCALE = float(HD) ** -0.5 * float(HEADS) ** -0.5
NEG_INADM, NEG_TAKEN, NEG_TEST = -3.0e38, -3.4e38, -3.3e38
MASKED = -1.0e30

G_CONV, G_QI, G_KI, G_K, G_Q, G_V = range(6)
GROUPS = [(2376, 512), (1536, 512), (2048, 328), (512, 512), (0, 512), (1024, 512)]
PIECES_GROUP = 4
PIECES_IN = PIECES_GROUP * len(GROUPS)
PIECES_MIX = PIECES_IN + 8
PIECES_E = 12
PIECES_L = PIECES_MIX + E * PIECES_E
RAW = 12
SHARE = 6
RING_E = 2 * RAW
SPL = 4
EXTRA = (TOPE * SEQ - E) // P
TILES = E + EXTRA
KEYS = [P * (b + 1) for b in range(TT)]
SC_AT = [None, 0, 256, 640]
SCORES = 1152
UNITS = TT * HEADS
TAPS_A = 18
TAPS_V = 2 * TAPS - TAPS_A
OUT_SPLIT = (8, 16, 24, 26)
VECS = TAPS + 5
V_DWB, V_LNG, V_LNB, V_PWB, V_PSC = range(TAPS, TAPS + 5)

C_ID, C_TRI, C_ONE, C_IOTA = 0, 128, 256, 384
C_REV, C_TOK, C_PW, C_PH = 512, 516, 520, 522
C_N = C_PH + 32

A_HROW = 0
A_QT, A_KT = 0, 2048
A_V = 4096
A_KI = 6144
A_P = A_KI
A_HPAD = 7168
A_ACC = A_HPAD + 2 * 542
A_SQ = A_ACC + 1024
A_U = A_SQ + 1024
A_UT = A_U + 2 * 528
A_SC = A_UT + 2 * 528
A_MB0 = A_SC + SCORES
A_L = A_MB0 + 128
A_PT = A_L + 1024
A_O = A_PT + 1024
A_N = A_O + 512
A_Y = A_L


def trunk(nc, t, out):
    with ExitStack() as ctx:
        def sb(name, shape, dt=F32):
            return ctx.enter_context(nc.sbuf_tensor(name, shape, dt))

        def sem(name):
            return ctx.enter_context(nc.semaphore(name))

        arena = sb("arena", [P, A_N])
        x = sb("x_sb", [P, TT, D])
        a_hi = sb("a_hi", [P, DC, SEQ], F32R)
        a_lo = sb("a_lo", [P, DC, SEQ], F32R)
        raw = sb("raw", [P, RAW, 1024])
        w_hi = sb("w_hi", [P, SPL, 1024], F32R)
        w_lo = sb("w_lo", [P, SPL, 1024], F32R)
        gain = sb("gain", [P, D])
        cst = sb("cst", [P, C_N])
        pw = sb("pw", [P, 2, CW])
        pbd = sb("pbd", [P, DEPTH, 2, P])
        rw = sb("rw", [P, DEPTH, DC, 20])
        rw_hi = sb("rw_hi", [P, DEPTH, DC, 20], F32R)
        rw_lo = sb("rw_lo", [P, DEPTH, DC, 20], F32R)
        rb = sb("rb", [P, DEPTH, 20])
        chan = sb("chan", [P, DEPTH, 2, VECS])
        widx = sb("widx", [P, TT, HEADS])
        top8 = sb("top8", [P, 3, 8])
        stat = sb("stat", [P, 3, UNITS])
        rinv = sb("rinv", [P, HEADS])
        nrm = sb("nrm", [P, 4, TT])
        tab = sb("tab", [P, TILES], I32)
        warm = sb("warm", [P, 2 + 2 * DEPTH])
        yidx = sb("yidx", [P, TT * TOPE], I32)
        ovx = sb("ovx", [P, EXTRA + 1], I32)
        gates = sb("gates", [P, TOPE, TT])

        ps = ctx.enter_context(nc.psum_tensor("ps", [P, 8, 512], F32))

        h2d = [nc.dram_tensor(f"h2_rows{l}", (SEQ, D), F32, kind="Internal").ap() for l in range(DEPTH)]
        yd = nc.dram_tensor("y_rows", (TILES * P, D), F32, kind="Internal").ap()

        def ar(at, n, *dims):
            v = arena[:, at:at + n]
            if len(dims) == 2:
                return v.rearrange("p (a n) -> p a n", a=dims[0])
            return v

        hrow = ar(A_HROW, 4096, TT, D)
        qT, kT = ar(A_QT, 2048, 4, SEQ), ar(A_KT, 2048, 4, SEQ)
        qiT, v_sb = ar(A_V, 2048, 4, SEQ), ar(A_V, 2048, 4, SEQ)
        kiT, wT = ar(A_KI, 512), ar(A_KI + 512, 512)
        hpad = ar(A_HPAD, 1084, 2, 542)
        acc = ar(A_ACC, 1024, 2, SEQ)
        sq = ar(A_SQ, 1024, 2, SEQ)
        u = ar(A_U, 1056, 2, 528)
        ut = ar(A_UT, 1056, 2, 528)
        mask = [arena[:, A_MB0:A_MB0 + P]] + [arena[:, A_SC + SC_AT[b]:A_SC + SC_AT[b] + KEYS[b]] for b in range(1, TT)]
        lsb = ar(A_L, 1024, 2, 512)
        prob = ar(A_P, 1024, 2, 512)
        pT = ar(A_PT, 1024, 2, 512)
        osb = ar(A_O, 512)
        product = ar(A_QT, 2048, 4, SEQ)
        vrows = ar(A_PT, DEPTH * CW, DEPTH, CW)
        pl = ln_t = hpad[:, :, 30:542]
        xg = [ar(A_V, D), gain[:]]
        slu, act = ar(A_V + 1024, HID), ar(A_V + 1536, HID)
        ysb = [[ar(A_Y, 512), ar(A_Y + 512, 512)], [ar(A_O, 512), pw[:].rearrange("p a n -> p (a n)")]]
        yc = [ar(at, D) for at in (A_HROW + 2 * D, A_HROW + 3 * D, A_P, A_ACC, A_SQ, A_V, A_V + D, A_PT)]
        squares = ar(A_L, D)
        lgT = ar(A_P, SEQ)
        slot_hot = ar(A_P, TT * TOPE * P, TT * TOPE, P)
        ident = cst[:, C_ID:C_ID + P]
        ones = cst[:, C_ONE:C_ONE + P]
        tri = cst[:, C_TRI:C_TRI + P]

        side = [acc, sq, hpad[:, :, 30:542], u[:, :, 16:528], ut[:, :, 16:528], pT] + [
            hrow[:, tt, :].rearrange("p (a n) -> p a n", a=2) for tt in range(TT)] + [
            ar(A_P, 1024, 2, 512), ar(A_SC, 1024, 2, 512)]
        SIDE_MIX, SIDE_ROWS = 6, 10

        at = A_SC
        R = {}
        for name, dims in (("lg", (TT, 20)), ("gd", (TT, 4)), ("ge", (TT, 4)), ("ei", (TT, 4)), ("t4", (TT, 4)), ("og", (TT, 4)),
                           ("fd", (TT, 4)), ("f2", (TT, 4)), ("o1", (TT, 4)), ("o2", (TT, 4)), ("mx", (TT,)), ("t1", (TT,)),
                           ("fx", (TT,)), ("fe", (TT,)), ("gs", (TT,)), ("den", (TT,)), ("pr", (TT, NG, NE)),
                           ("m12", (TOPE, TT, E)), ("ms", ((TT + 1) * E,)), ("tm", (TOPE, TT, E)), ("tb", (TOPE, TT, E)),
                           ("p2", (TOPE, TT)), ("b2", (TOPE, TT)), ("e2", (TOPE, TT)), ("k2", (TOPE, TT)), ("v2", (TOPE, TT)),
                           ("c2", (TOPE, TT)), ("d2", (TOPE, TT)), ("ex", (E,)), ("cum", (E,)), ("base", (E,)), ("oe", (EXTRA,)),
                           ("hot", (TT * TOPE, TILES))):
            n = int(np.prod(dims))
            view = arena[:, at:at + n]
            letters = "abc"[:len(dims)]
            if len(dims) > 1:
                view = view.rearrange(f"p ({' '.join(letters)}) -> p {' '.join(letters)}",
                                      **dict(zip(letters[:-1], dims[:-1])))
            R[name] = view
            at += n
        R["cmp"] = R["tb"].rearrange("p a b c -> p (a b c)")[:, 0:EXTRA * E].rearrange("p (j e) -> p j e", j=EXTRA)
        assert at <= A_SC + SCORES, at
        head = sb("head", [P, 2, 16])[:]

        cst_in, chan_in, rout_in, pbd_in, x_in, pads = sem("cst_in"), sem("chan_in"), sem("rout_in"), sem("pbd_in"), [sem(f"x_in{tt}") for tt in range(TT)], sem("pads")
        chan_t, chan_set, rw_split = sem("chan_t"), sem("chan_set"), sem("rw_split")
        dve_step = sem("dve_step")
        raw_in = [sem(f"raw_in{s}") for s in range(RAW)]
        side_in = [sem(f"side_in{s}") for s in range(0, RING_E - RAW, SHARE)]
        w_hi_set, w_lo_set, w_used = sem("w_hi_set"), sem("w_lo_set"), sem("w_used")
        gain_in, ssq_set, ms_set, rms_set, hrow_set = (sem(n) for n in ("gain_in", "ssq_set", "ms_set", "rms_set", "hrow_set"))
        ht_ready, ht_hi, ht_lo = sem("ht_ready"), sem("ht_hi"), sem("ht_lo")
        proj_ready = sem("proj_ready")
        qi_set, ki_set, u_set, sig_set, glu_set, k_set, q_set, v_set = (
            sem(n) for n in ("qi_set", "ki_set", "u_set", "sig_set", "glu_set", "k_set", "q_set", "v_set"))
        wt_ready, widx_set, dots_ready, relu_set, idx_acc, inadm_set, topk_step = (
            sem(n) for n in ("wt_ready", "widx_set", "dots_ready", "relu_set", "idx_acc", "inadm_set", "topk_step"))
        conv_mul, conv_sum, conv_tap, pool_d, pw_in = sem("conv_mul"), sem("conv_sum"), sem("conv_tap"), sem("pool_d"), sem("pw_in")
        qk_ready, logit_set, negmax_set, exp_set, pt_ready, pt_set, pv_ready, o_set, ot_ready = (
            sem(n) for n in ("qk_ready", "logit_set", "negmax_set", "exp_set", "pt_ready", "pt_set", "pv_ready", "o_set", "ot_ready"))
        pool_ready, mean_ready, ln_d, ln_sq, var_ready, ln_ms, ln_rms, ln_n, ln_y, pw_ready = (
            sem(n) for n in ("pool_ready", "mean_ready", "ln_d", "ln_sq", "var_ready", "ln_ms", "ln_rms", "ln_n", "ln_y", "pw_ready"))
        o_hi_set, o_lo_set, pw_hi, pw_lo, pool_hi, pool_lo = (
            sem(n) for n in ("o_hi_set", "o_lo_set", "pw_hi", "pw_lo", "pool_hi", "pool_lo"))
        out_ready, x_mixed = sem("out_ready"), sem("x_mixed")
        rlog_ready, lgt_set, rtok_ready, exp_in, exp_out, route_set, pos_ready, hot_set, tab_ready, tab_set, ovx_set = (
            sem(n) for n in ("rlog_ready", "lgt_set", "rtok_ready", "exp_in", "exp_out", "route_set", "pos_ready", "hot_set",
                             "tab_ready", "tab_set", "ovx_set"))
        y_zero = sem("y_zero")
        h2_stored = sem("h2_stored")
        yc_in = [sem(f"yc_in{q}") for q in range(TT * TOPE)]
        x_moe, out_done = sem("x_moe"), sem("out_done")

        class Tiles:
            def __init__(self, tag, own_ring):
                self.xg_in = [sem(f"xg_in{h}{tag}") for h in range(1 if own_ring else 2)]
                self.xt_ready = sem(f"xt_ready{tag}")
                self.xt_hi = sem(f"xt_hi{tag}")
                self.xt_lo = sem(f"xt_lo{tag}")
                self.silu_set = sem(f"silu_set{tag}")
                self.act_set = sem(f"act_set{tag}")
                self.at_ready = sem(f"at_ready{tag}")
                self.at_hi = sem(f"at_hi{tag}")
                self.at_lo = sem(f"at_lo{tag}")
                self.y_set_a = sem(f"y_set_a{tag}")
                self.y_set_v = sem(f"y_set_v{tag}")
                self.y_stored = [sem(f"y_stored{h}{tag}") for h in range(1 if own_ring else 2)]
                if own_ring:
                    self.raw_in = [sem(f"raw_in{s}{tag}") for s in range(0, SPL, 2)]
                    self.w_hi_set, self.w_lo_set, self.w_used = sem(f"w_hi_set{tag}"), sem(f"w_lo_set{tag}"), sem(f"w_used{tag}")
                else:
                    self.raw_in, self.w_hi_set, self.w_lo_set, self.w_used = raw_in, w_hi_set, w_lo_set, w_used

        main = Tiles("", False)
        over = [Tiles(f"_over{l}", True) for l in range(DEPTH)]

        def cnt(i, per, c):
            return c if i is None else i * per + c

        slot_of, turn, before = [], [], []
        for n in range(DEPTH * PIECES_L):
            m = n % PIECES_L
            slot = (m - PIECES_MIX) % RAW if m < PIECES_MIX else (m - PIECES_MIX) % RING_E
            same = [k for k in range(n) if slot_of[k] == slot]
            slot_of.append(slot)
            turn.append(len(same) + 1)
            before.append(same[-1] if same else None)

        def place(S, i, n, w=1024):
            if S is not main:
                slot = n % SPL
            else:
                slot = slot_of[n if i is None else n + 2 * RING_E]
            if slot >= RAW:
                return side[slot - RAW]
            return raw[:, slot, 0:w].rearrange("p (a n) -> p a n", a=2)

        def landed(S, i, n):
            if S is not main:
                return S.raw_in[n % SPL // 2], 64 * (n // SPL + 1)
            m = n if i is None else n + 2 * RING_E
            back = 0 if i is None else 2
            if slot_of[m] < RAW:
                return raw_in[slot_of[m]], cnt(i, 32, 32 * (turn[m] - back))
            return side_in[(slot_of[m] - RAW) // SHARE], cnt(i, 32 * SHARE, 32 * SHARE * (turn[m] - back))

        def load(sp, S, i, n, sources, w=1024):
            if S is not main:
                last = n - SPL
            elif i is None:
                last = before[n]
            else:
                last = before[n + 2 * RING_E] - 2 * RING_E
            if last is not None and (i is not None or last >= 0):
                sp.wait_ge(S.w_lo_set, cnt(i, RING_E, last + 1))
            dst = place(S, i, n, w)
            for a, src in enumerate(sources):
                sp.dma_start(dst[:, a, :], src).then_inc(landed(S, i, n)[0], 16)

        def load_in(sp, l, n, g, j):
            c0, w = GROUPS[g]
            load(sp, main, None, n, [t["w_in"][l, (2 * j + a) * P:(2 * j + a + 1) * P, c0:c0 + w] for a in range(2)], 2 * w)

        def load_out(sp, l, n, j):
            load(sp, main, None, n, [t["w_out"][l, j * P:(j + 1) * P, a * 512:(a + 1) * 512] for a in range(2)])

        def load_gu(sp, S, l, i, n, e, c):
            load(sp, S, i, n, [t[w][bass.ds(e + l * E, 1), c * P:(c + 1) * P, :].rearrange("a p n -> (a p) n")
                               for w in ("w_gate", "w_up")])

        def load_down(sp, S, l, i, n, e, j):
            load(sp, S, i, n, [t["w_down"][bass.ds(e + l * E, 1), j * P:(j + 1) * P, a * 512:(a + 1) * 512]
                               .rearrange("a p n -> (a p) n") for a in range(2)])

        def split_slot(w_part, n, w):
            return w_part[:, n % SPL, 0:w].rearrange("p (a n) -> p a n", a=2)

        def hi(eng, S, i, n, w=1024):
            eng.wait_ge(*landed(S, i, n))
            if i is not None or n >= SPL:
                eng.wait_ge(S.w_used, cnt(i, RING_E, n - SPL + 1))
            nc.scalar.activation(split_slot(w_hi, n, w), place(S, i, n, w), ACT.Copy).then_inc(S.w_hi_set, 1)

        def lo(eng, S, i, n, w=1024):
            eng.wait_ge(S.w_hi_set, cnt(i, RING_E, n + 1))
            nc.vector.tensor_tensor(split_slot(w_lo, n, w), place(S, i, n, w), split_slot(w_hi, n, w).bitcast(F32),
                                    ALU.subtract).then_inc(S.w_lo_set, 1)

        def use(pe, S, i, n):
            pe.wait_ge(S.w_lo_set, cnt(i, RING_E, n + 1))

        def three(o, lh, ll, rh, rl, start, stop):
            nc.tensor.matmul(o, lh, rh, start=start, stop=False)
            nc.tensor.matmul(o, lh, rl, start=False, stop=False)
            return nc.tensor.matmul(o, ll, rh, start=False, stop=stop)

        def bank_ready(eng, l, g, m):
            banks = 3 if g == G_KI else 4
            if m == banks - 1:
                eng.wait_ge(w_used, l * PIECES_L + (g + 1) * PIECES_GROUP)
            else:
                eng.wait_ge(proj_ready, 17 * l + 3 * g - (g > G_KI) + m + 1)

        def rows_of(S, l, i, e):
            if S is not main:
                return xg[0], S.xg_in[0], 16 * (e + 1)
            earlier = (E // 2 + 1 if e % 2 == 0 else E // 2) * l
            return xg[e % 2], S.xg_in[e % 2], cnt(i, 16, 16 * (earlier + e // 2 + 1))

        def y_of(S, l, i, e):
            if S is not main:
                return ysb[0], S.y_stored[0], 32 * e
            return ysb[e % 2], S.y_stored[e % 2], cnt(i, 32, 32 * (E // 2 * l + e // 2))

        def all_stored(eng, l):
            for there in main.y_stored:
                eng.wait_ge(there, 32 * (E // 2) * (l + 1))

        block = ctx.enter_context(nc.Block())

        @block.sync
        def _(sp):
            for tt in range(TT):
                sp.dma_start(x[:, tt, :], t["x"][0, tt * P:(tt + 1) * P, :]).then_inc(x_in[tt], 16)
            for l in range(DEPTH):
                n = l * PIECES_L
                for g in range(len(GROUPS)):
                    for j in range(PIECES_GROUP):
                        if l and g == 1 and j == 0:
                            sp.wait_ge(yc_in[TT * TOPE - 1], 16 * l)
                        load_in(sp, l, n, g, j)
                        n += 1
                for j in range(8):
                    load_out(sp, l, n, j)
                    n += 1

                def load_expert_piece(k):
                    e, c = ((k - 8) // PIECES_E, (k - 8) % PIECES_E) if k >= 8 else (-1, k)
                    if c < 8:
                        load_gu(sp, main, l, None, n + k, e + 1, c)
                    else:
                        load_down(sp, main, l, None, n + k, e, c - 8)

                for k in range(RAW):
                    load_expert_piece(k)
                sp.wait_ge(x_mixed, 8 * (l + 1))
                if l == 0:
                    sp.wait_ge(y_zero, 16 * EXTRA)
                for k in range(RAW, RAW + SIDE_MIX):
                    load_expert_piece(k)
                sp.wait_ge(h2_stored, 16 * TT * (l + 1))
                sp.wait_ge(ht_ready, 2 * DC * (l + 1))
                for k in range(RAW + SIDE_MIX, RAW + SIDE_ROWS):
                    load_expert_piece(k)
                for k in range(RING_E, RING_E + SPL):
                    load_expert_piece(k)
                sp.wait_ge(tab_set, l + 1)
                sp.wait_ge(ovx_set, l + 1)
                for k in (*range(RAW + SIDE_ROWS, RING_E), *range(RING_E + SPL, 8 + 3 * PIECES_E)):
                    load_expert_piece(k)
                n += 8 - PIECES_E
                with sp.Fori(2, E // 2) as i:
                    for d in range(2):
                        for c in range(8):
                            load_gu(sp, main, l, i, n + d * PIECES_E + c, i * 2 + d, c)
                        for j in range(4):
                            load_down(sp, main, l, i, n + d * PIECES_E + 8 + j, i * 2 + (d - 1), j)
                n += PIECES_E * E
                for j in range(4):
                    load_down(sp, main, l, None, n + j, E - 1, j)
                n += 4
                sp.wait_ge(ovx_set, l + 1)
                extra = sp.value_load(ovx[0:1, EXTRA:EXTRA + 1], min_val=0, max_val=EXTRA)
                with sp.If(extra > 0):
                    sp.wait_ge(main.w_lo_set, n)
                    for j in range(EXTRA):
                        e = sp.value_load(ovx[0:1, j:j + 1], min_val=0, max_val=E - 1)
                        for c in range(8):
                            load_gu(sp, over[l], l, None, j * PIECES_E + c, e, c)
                        for d in range(4):
                            load_down(sp, over[l], l, None, j * PIECES_E + 8 + d, e, d)
                    sp.wait_ge(over[l].w_lo_set, EXTRA * PIECES_E)
            for tt in range(TT):
                sp.wait_ge(hrow_set, 2 * DEPTH * TT + tt + 1)
                sp.dma_start(out[0, tt * P:(tt + 1) * P, :], hrow[:, tt, :]).then_inc(out_done, 16)
            sp.wait_ge(out_done, 16 * TT)

        @block.gpsimd
        def _(pool):
            g = nc.gpsimd
            g.memset(warm[:], 1.0).then_inc(pads, 1)

            def gain_load(k):
                src = t["final_g"] if k == 2 * DEPTH else t["norm2_g" if k % 2 else "norm1_g"][k // 2]
                pool.dma_start(gain[:], src.partition_broadcast(P)).then_inc(gain_in, 16)

            gain_load(0)
            pool.dma_start(cst[:], t["shape_constants"]).then_inc(cst_in, 16)
            pool.dma_start(vrows[0:TAPS], t["dw_w"].rearrange("l k c -> k l c")).then_inc(chan_in, 16)
            for row, name in ((V_DWB, "dw_b"), (V_LNG, "conv_ln_g"), (V_LNB, "conv_ln_b"), (V_PWB, "pw_b"), (V_PSC, "pool_scale")):
                pool.dma_start(vrows[row:row + 1], t[name].unsqueeze(0)).then_inc(chan_in, 16)
            for v in (hpad[:, :, 0:30], u[:, :, 0:16], ut[:, :, 0:16], pbd[:], acc):
                g.memset(v, 0.0).then_inc(pads, 1)
            g.memset(mask[0], 0.0).then_inc(pads, 1)
            pool.wait_ge(pads, 7)
            g.memset(arena[0:CHUNK, A_MB0 + CHUNK:A_MB0 + P], MASKED).then_inc(pads, 1)
            pool.dma_start(rb[:, :, 0:NG], t["rg_b"].partition_broadcast(P)).then_inc(rout_in, 16)
            pool.dma_start(rb[:, :, NG:20], t["re_b"].partition_broadcast(P)).then_inc(rout_in, 16)
            for l in range(DEPTH):
                pool.dma_start(rw[:, l, :, 0:NG], t["rg_w"][l].rearrange("(c p) n -> p c n", p=P),
                               allow_slow_non_contiguous=True).then_inc(rout_in, 16)
                pool.dma_start(rw[:, l, :, NG:20], t["re_w"][l].rearrange("(c p) n -> p c n", p=P),
                               allow_slow_non_contiguous=True).then_inc(rout_in, 16)
                for h in range(2):
                    pool.dma_start(pbd[h * 64:(h + 1) * 64, l, :, h * 64:(h + 1) * 64],
                                   t["pool_w"][l, h::2].rearrange("g c d -> c g d")).then_inc(pbd_in, 16)
            for j in range(EXTRA):
                pool.dma_start(yd[(E + j) * P:(E + j + 1) * P, :], acc.rearrange("p a n -> p (a n)")).then_inc(y_zero, 16)

            for l in range(DEPTH):
                if l:
                    pool.wait_ge(pw_ready, 2 * l)
                pool.dma_start(pw[:], t["pw_w"][l].rearrange("(c p) n -> p c n", p=P)).then_inc(pw_in, 16)
                for k in range(1, TAPS_A):
                    pool.wait_ge(conv_mul, TAPS_A * l + k + 1)
                    if k >= 2:
                        pool.wait_ge(conv_sum, (TAPS_A - 1) * l + k - 1)
                    g.tensor_tensor(acc[:, 0, :], acc[:, 0, :], product[:, k % 4, :], ALU.add).then_inc(conv_sum, 1)
                k = 2 * l + 1
                pool.wait_ge(hrow_set, 4 * k)
                gain_load(k)
                for tt in range(TT):
                    pool.wait_ge(hrow_set, 4 * k + tt + 1)
                    pool.dma_start(h2d[l][tt * P:(tt + 1) * P, :], hrow[:, tt, :]).then_inc(h2_stored, 16)
                pool.wait_ge(tab_set, l + 1)
                pool.wait_ge(h2_stored, 16 * TT * (l + 1))

                def gather(S, col, e, done):
                    if done > 0:
                        pool.wait_ge(S.xt_ready, 2 * done)
                    rows, there, _ = rows_of(S, l, None, e)
                    pool.indirect_dma_start(rows, None, h2d[l], bass.IndirectOffsetOnAxis(ap=tab[:, col:col + 1], axis=0)
                                            ).then_inc(there, 16)

                def store(S, tile, i, c):
                    pool.wait_ge(S.y_set_a, cnt(i, 2, c))
                    pool.wait_ge(S.y_set_v, cnt(i, 2, c))
                    rows, there, _ = y_of(S, l, None, tile if S is main else tile - E)
                    for h in range(2):
                        pool.dma_start(yd[tile * P:(tile + 1) * P, h * 512:(h + 1) * 512], rows[h]).then_inc(there, 16)

                for e in range(E + 1):
                    gather(main, e, e, (E + 1) * l + e - 1 if e >= 2 else (E + 1) * l)
                    if e >= 4:
                        store(main, e - 4, None, E * l + e - 3)
                pool.wait_ge(main.xt_ready, 2 * ((E + 1) * l + E))
                gain_load(k + 1)
                for e in range(E - 3, E):
                    store(main, e, None, E * l + e + 1)
                pool.wait_ge(ovx_set, l + 1)
                extra = pool.value_load(ovx[0:1, EXTRA:EXTRA + 1], min_val=0, max_val=EXTRA)
                with pool.If(extra > 0):
                    pool.wait_ge(y_zero, 16 * EXTRA)
                    pool.wait_ge(main.xt_ready, 2 * (E + 1) * (l + 1))
                    for j in range(EXTRA):
                        gather(over[l], E + j, j, j)
                        store(over[l], E + j, None, j + 1)
                    pool.wait_ge(over[l].y_stored[0], 32 * EXTRA)
                if l == 0:
                    pool.wait_ge(y_zero, 16 * EXTRA)
                all_stored(pool, l)
                pool.wait_ge(main.xt_ready, 2 * (E + 1) * (l + 1))
                for q in range(TT * TOPE):
                    pool.indirect_dma_start(yc[q], None, yd, bass.IndirectOffsetOnAxis(ap=yidx[:, q:q + 1], axis=0)
                                            ).then_inc(yc_in[q], 16)

        @block.tensor
        def _(pe):
            T = nc.tensor

            def norm_transposes(k):
                for tt in range(TT):
                    pe.wait_ge(hrow_set, 4 * k + tt + 1)
                    for c in range(DC):
                        if k % 2 and tt == 0:
                            pe.wait_ge(x_mixed, 8 * (k // 2) + c + 1)
                        mm = T.transpose(ps[:, c, tt * P:(tt + 1) * P], hrow[:, tt, c * P:(c + 1) * P], ident)
                        if tt == TT - 1:
                            mm.then_inc(ht_ready, 1)

            def project(l, g, banks):
                w = GROUPS[g][1]
                cols = [(0, 72), (72, P), (200, P)] if g == G_KI else [(m * P, P) for m in range(4)]
                n = l * PIECES_L + g * PIECES_GROUP
                for j in range(PIECES_GROUP):
                    use(pe, main, None, n + j)
                    if g == G_CONV:
                        pe.wait_ge(ht_lo, 16 * l + (4 if j == 0 else 2 * (j + 1)))
                    for a in range(2):
                        c = 2 * j + a
                        s = (n + j) % SPL
                        for m, (c0, M) in enumerate(cols):
                            if g == G_V:
                                tk = slice(m * P, (m + 1) * P)
                                mm = three(ps[:, banks[m], :], a_hi[:, c, tk], a_lo[:, c, tk],
                                           w_hi[:, s, a * w:(a + 1) * w], w_lo[:, s, a * w:(a + 1) * w], c == 0, c == DC - 1)
                            else:
                                k0 = a * w + c0
                                mm = three(ps[0:M, banks[m], :], w_hi[:, s, k0:k0 + M], w_lo[:, s, k0:k0 + M],
                                           a_hi[:, c, :], a_lo[:, c, :], c == 0, c == DC - 1)
                            if j == PIECES_GROUP - 1 and a == 1 and m < len(cols) - 1:
                                mm.then_inc(proj_ready, 1)
                    mm.then_inc(w_used, 1)

            def router(l):
                pe.wait_ge(rw_split, 1)
                for c in range(DC):
                    pe.wait_ge(ht_lo, 16 * l + 8 + c + 1)
                    mm = three(ps[0:20, 0, :], rw_hi[:, l, c, :], rw_lo[:, l, c, :], a_hi[:, c, :], a_lo[:, c, :],
                               c == 0, c == DC - 1)
                mm.then_inc(rlog_ready, 1)
                pe.wait_ge(lgt_set, l + 1)
                for tt in range(TT):
                    mm = T.transpose(ps[:, 1, tt * 32:tt * 32 + 20], lgT[0:20, tt * P:(tt + 1) * P], cst[0:20, C_ID:C_ID + 20])
                mm.then_inc(rtok_ready, 1)
                pe.wait_ge(route_set, l + 1)
                T.matmul(ps[:, 2, 0:(TT + 1) * E], tri, R["ms"], start=True, stop=False)
                for s in range(1, TT + 1):
                    mm = T.matmul(ps[:, 2, s * E:(TT + 1) * E], ones, R["ms"][:, 0:(TT + 1 - s) * E], start=False, stop=s == TT)
                mm.then_inc(pos_ready, 1)
                for q in range(TT * TOPE):
                    pe.wait_ge(hot_set, TT * TOPE * l + q + 1)
                    mm = T.matmul(ps[:, 3, 0:TILES], slot_hot[:, q, :], R["hot"][:, q, :], start=(q == 0), stop=(q == TT * TOPE - 1))
                mm.then_inc(tab_ready, 1)

            def tile_rows(S, l, i, c, e):
                rows, there, count = rows_of(S, l, i, e)
                pe.wait_ge(there, count)
                if i is not None or c:
                    pe.wait_ge(S.xt_lo, cnt(i, 4, 2 * c))
                for h in range(2):
                    for q in range(4):
                        mm = T.transpose(ps[:, 2 + h, q * P:(q + 1) * P], rows[:, (4 * h + q) * P:(4 * h + q + 1) * P], ident)
                    mm.then_inc(S.xt_ready, 1)

            def tile_gu(S, i, c, n, xc):
                pe.wait_ge(S.xt_lo, cnt(i, 4, 2 * (xc + 1)))
                if i is not None or c:
                    pe.wait_ge(S.act_set, cnt(i, 2, c))
                for k in range(8):
                    use(pe, S, i, n + k)
                    s = (n + k) % SPL
                    for h in range(2):
                        mm = three(ps[:, h, :], a_hi[:, k, 0:P], a_lo[:, k, 0:P],
                                   w_hi[:, s, h * 512:(h + 1) * 512], w_lo[:, s, h * 512:(h + 1) * 512], k == 0, k == 7)
                    mm.then_inc(S.w_used, 1)

            def tile_act(S, i, c):
                pe.wait_ge(S.act_set, cnt(i, 2, c + 1))
                for q in range(4):
                    mm = T.transpose(ps[:, 4, q * P:(q + 1) * P], act[:, q * P:(q + 1) * P], ident)
                mm.then_inc(S.at_ready, 1)

            def tile_down(S, i, c, n):
                pe.wait_ge(S.at_lo, cnt(i, 2, c + 1))
                if i is not None or c:
                    pe.wait_ge(S.y_set_a, cnt(i, 2, c))
                    pe.wait_ge(S.y_set_v, cnt(i, 2, c))
                for k in range(4):
                    use(pe, S, i, n + k)
                    s = (n + k) % SPL
                    for h in range(2):
                        mm = three(ps[:, 5 + h, :], a_hi[:, k, P:2 * P], a_lo[:, k, P:2 * P],
                                   w_hi[:, s, h * 512:(h + 1) * 512], w_lo[:, s, h * 512:(h + 1) * 512], k == 0, k == 3)
                    mm.then_inc(S.w_used, 1)

            def channel_columns():
                pe.wait_ge(chan_in, 16 * 6)
                for l in range(DEPTH):
                    for h in range(2):
                        mm = T.transpose(ps[:, 4, (2 * l + h) * VECS:(2 * l + h + 1) * VECS],
                                         vrows[0:VECS, l, h * P:(h + 1) * P], cst[0:VECS, C_ID:C_ID + VECS])
                mm.then_inc(chan_t, 1)
                pe.wait_ge(chan_set, 1)

            pe.wait_ge(cst_in, 16)
            for l in range(DEPTH):
                norm_transposes(2 * l)
                project(l, G_CONV, [0, 1, 2, 3])
                if l == 0:
                    channel_columns()
                project(l, G_QI, [4, 5, 6, 7])
                pe.wait_ge(glu_set, 2 * (l + 1))
                project(l, G_KI, [0, 1, 2])
                pe.wait_ge(ki_set, 3 * (l + 1))
                for tt in range(TT):
                    mm = T.transpose(ps[:, 3, tt * HEADS:(tt + 1) * HEADS], wT[64:72, tt * P:(tt + 1) * P],
                                     cst[64:72, C_ID + 64:C_ID + 72])
                mm.then_inc(wt_ready, 1)
                pe.wait_ge(qi_set, 4 * (l + 1))
                for v in range(24):
                    h, b = v // 3, v % 3 + 1
                    r = slice((h % 2) * 64, (h % 2) * 64 + 64)
                    if v >= 4:
                        pe.wait_ge(relu_set, 24 * l + v - 3)
                    T.matmul(ps[:, 4 + v % 4, 0:KEYS[b]], qiT[r, h // 2, b * P:(b + 1) * P], kiT[r, 0:KEYS[b]],
                             start=True, stop=True).then_inc(dots_ready, 1)
                pe.wait_ge(u_set, 2 * (l + 1))
                pe.wait_ge(widx_set, l + 1)
                project(l, G_K, [0, 1, 2, 3])
                pe.wait_ge(relu_set, 24 * (l + 1))
                project(l, G_Q, [4, 5, 6, 7])
                pe.wait_ge(k_set, 4 * (l + 1))
                project(l, G_V, [0, 1, 2, 3])

                pe.wait_ge(q_set, 4 * (l + 1))

                def turn_o(b):
                    pe.wait_ge(o_set, TT * l + b + 1)
                    if b:
                        pe.wait_ge(o_lo_set, TT * l + b)
                    for j in range(4):
                        mm = T.transpose(ps[:, 2, j * P:(j + 1) * P], osb[:, j * P:(j + 1) * P], ident)
                    mm.then_inc(ot_ready, 1)

                def other(s):
                    if s == 5:
                        pe.wait_ge(conv_tap, TAPS_V * (l + 1))
                        for m in range(2):
                            mm = T.matmul(ps[:, 3, :], ones, acc[:, m, :], start=(m == 0), stop=(m == 1))
                        mm.then_inc(mean_ready, 1)
                    if s == 9:
                        pe.wait_ge(ln_sq, 2 * (l + 1))
                        for m in range(2):
                            mm = T.matmul(ps[:, 3, :], ones, sq[:, m, :], start=(m == 0), stop=(m == 1))
                        mm.then_inc(var_ready, 1)
                    if s in (16, 19):
                        m = (16, 19).index(s)
                        if m == 0:
                            pe.wait_ge(ln_y, 2 * (l + 1))
                            pe.wait_ge(pw_in, 16 * (l + 1))
                        else:
                            pe.wait_ge(pw_lo, 2 * l + 1)
                        for c in range(2):
                            mm = T.matmul(ps[:, 3, :], pw[:, c, m * P:(m + 1) * P], sq[:, c, :], start=(c == 0), stop=(c == 1))
                        mm.then_inc(pw_ready, 1)
                    if s in (27, 30):
                        m = (27, 30).index(s)
                        if m == 0:
                            pe.wait_ge(pw_lo, 2 * (l + 1))
                            pe.wait_ge(pool_d, l + 1)
                            pe.wait_ge(pbd_in, 16 * 2 * DEPTH)
                        else:
                            pe.wait_ge(pool_lo, 2 * l + 1)
                        T.matmul(ps[:, 3, :], pbd[:, l, m, :], ut[:, m, 16:528], start=True, stop=True).then_inc(pool_ready, 1)

                for s in range(UNITS + 2):
                    if s < UNITS:
                        b, h = s // HEADS, s % HEADS
                        r = slice((h % 2) * 64, (h % 2) * 64 + 64)
                        if s >= 2:
                            pe.wait_ge(logit_set, UNITS * l + s - 1)
                        T.matmul(ps[:, 4 + s % 2, 0:KEYS[b]], qT[r, h // 2, b * P:(b + 1) * P], kT[r, h // 2, 0:KEYS[b]],
                                 start=True, stop=True).then_inc(qk_ready, 1)
                    if 1 <= s <= UNITS:
                        w = s - 1
                        pe.wait_ge(exp_set, UNITS * l + w + 1)
                        if w >= 2:
                            pe.wait_ge(pt_set, UNITS * l + w - 1)
                        for kb in range(w // HEADS + 1):
                            mm = T.transpose(ps[:, 6 + w % 2, kb * P:(kb + 1) * P], prob[:, w % 2, kb * P:(kb + 1) * P], ident)
                        mm.then_inc(pt_ready, 1)
                    other(s)
                    if s >= 2:
                        w = s - 2
                        b, h = w // HEADS, w % HEADS
                        if w == 0:
                            pe.wait_ge(v_set, 4 * (l + 1))
                        pe.wait_ge(pt_set, UNITS * l + w + 1)
                        if h == 0 and b >= 2:
                            pe.wait_ge(o_set, TT * l + b - 1)
                        for kb in range(b + 1):
                            mm = T.matmul(ps[:, b % 2, h * HD:(h + 1) * HD], pT[:, w % 2, kb * P:(kb + 1) * P],
                                          v_sb[:, kb, h * HD:(h + 1) * HD], start=(kb == 0), stop=(kb == b))
                        mm.then_inc(pv_ready, 1)
                    if s >= 11 and (s - 11) % HEADS == 0:
                        turn_o((s - 11) // HEADS)
                turn_o(TT - 1)
                pe.wait_ge(pool_lo, 2 * (l + 1))
                pe.wait_ge(o_lo_set, TT * (l + 1))
                n = l * PIECES_L + PIECES_IN
                for j in range(8):
                    use(pe, main, None, n + j)
                    s = (n + j) % SPL
                    for tt in range(TT):
                        for h in range(2):
                            tk = slice(tt * P, (tt + 1) * P)
                            mm = three(ps[:, 2 * tt + h, :], a_hi[:, j, tk], a_lo[:, j, tk],
                                       w_hi[:, s, h * 512:(h + 1) * 512], w_lo[:, s, h * 512:(h + 1) * 512], j == 0, j == 7)
                            if j == 7 and 2 * tt + h < 7:
                                mm.then_inc(out_ready, 1)
                    mm.then_inc(w_used, 1)

                norm_transposes(2 * l + 1)
                router(l)
                n = l * PIECES_L + PIECES_MIX
                te, tx = E * l, (E + 1) * l
                tile_rows(main, l, None, tx, 0)
                tile_gu(main, None, te, n, tx)
                tile_rows(main, l, None, tx + 1, 1)
                tile_act(main, None, te)
                n += 8

                def step(i, e):
                    m = n + e * PIECES_E
                    tile_gu(main, i, te + e + 1, m, tx + e + 1)
                    tile_rows(main, l, i, tx + e + 2, e + 2)
                    tile_down(main, i, te + e, m + 8)
                    tile_act(main, i, te + e + 1)

                step(None, 0)
                with pe.Fori(1, E // 2) as i:
                    step(i, -1)
                    step(i, 0)
                tile_down(main, None, te + E - 1, n + PIECES_E * (E - 1))
                pe.wait_ge(ovx_set, l + 1)
                extra = pe.value_load(ovx[0:1, EXTRA:EXTRA + 1], min_val=0, max_val=EXTRA)
                with pe.If(extra > 0):
                    pe.wait_ge(main.xt_lo, 2 * (tx + E + 1))
                    pe.wait_ge(main.y_set_a, te + E)
                    pe.wait_ge(main.y_set_v, te + E)
                    for j in range(EXTRA):
                        tile_rows(over[l], l, None, j, j)
                        tile_gu(over[l], None, j, j * PIECES_E, j)
                        tile_act(over[l], None, j)
                        tile_down(over[l], None, j, j * PIECES_E + 8)

        @block.scalar
        def _(sc):
            A = nc.scalar

            def norm_act(k, ready):
                A.activation(warm[:, 1 + k:2 + k], warm[:, 0:1], ACT.Sqrt)
                for tt in range(TT + 1):
                    if tt < TT:
                        ready(tt)
                        if k or tt:
                            sc.wait_ge(ssq_set, TT * k + tt)
                        A.activation(squares, x[:, tt, :], ACT.Square, accum_out=nrm[:, 0, tt:tt + 1]).then_inc(ssq_set, 1)
                    if tt:
                        sc.wait_ge(ms_set, TT * k + tt)
                        A.activation(nrm[:, 2, tt - 1:tt], nrm[:, 1, tt - 1:tt], ACT.Sqrt).then_inc(rms_set, 1)

            def norm_hi(k):
                for c in range(DC):
                    sc.wait_ge(ht_ready, DC * k + c + 1)
                    A.activation(a_hi[:, c, :], ps[:, c, :], ACT.Copy).then_inc(ht_hi, 1)

            def tile_xt(S, i, c):
                for h in range(2):
                    sc.wait_ge(S.xt_ready, cnt(i, 4, 2 * c + h + 1))
                    A.activation(a_hi[:, 4 * h:4 * h + 4, 0:P], ps[:, 2 + h, :].rearrange("p (q n) -> p q n", q=4),
                                 ACT.Copy).then_inc(S.xt_hi, 1)

            def tile_silu(S, i, n):
                sc.wait_ge(S.w_used, cnt(i, RING_E, n + 8))
                A.activation(slu, ps[:, 0, :], ACT.Silu).then_inc(S.silu_set, 1)

            def tile_at(S, i, c):
                sc.wait_ge(S.at_ready, cnt(i, 2, c + 1))
                A.activation(a_hi[:, 0:4, P:2 * P], ps[:, 4, :].rearrange("p (q n) -> p q n", q=4),
                             ACT.Copy).then_inc(S.at_hi, 1)

            def tile_y(S, l, i, e, n):
                sc.wait_ge(S.w_used, cnt(i, RING_E, n + 4))
                rows, there, free = y_of(S, l, i, e)
                if i is not None or free:
                    sc.wait_ge(there, free)
                A.activation(rows[0], ps[:, 5, :], ACT.Copy).then_inc(S.y_set_a, 1)

            for l in range(DEPTH):
                n0 = l * PIECES_L
                if l == 0:
                    sc.wait_ge(pads, 1)
                else:
                    for j in range(4):
                        hi(sc, main, None, n0 + j)
                norm_act(2 * l, (lambda tt: sc.wait_ge(x_in[tt], 16)) if l == 0 else
                         (lambda tt: sc.wait_ge(x_moe, 2 * TT * (l - 1) + 2 * (tt + 1))))
                if l == 0:
                    for j in range(4):
                        hi(sc, main, None, j)
                norm_hi(2 * l)
                for j in range(4, 8):
                    hi(sc, main, None, n0 + j)
                for m in range(2):
                    bank_ready(sc, l, G_CONV, 2 + m)
                    A.activation(lsb[:, m, :], ps[:, 2 + m, :], ACT.Sigmoid).then_inc(sig_set, 1)

                def taps(a, b):
                    for k in range(a, b):
                        src, w = hpad[:, 0, k:k + SEQ], chan[:, l, 0, k:k + 1]
                        if k == 0:
                            sc.wait_ge(glu_set, 2 * l + 1)
                            if l == 0:
                                sc.wait_ge(y_zero, 16 * EXTRA)
                            A.activation(acc[:, 0, :], src, ACT.Identity, scale=w,
                                         bias=chan[:, l, 0, V_DWB:V_DWB + 1]).then_inc(conv_mul, 1)
                        else:
                            if k >= 5:
                                sc.wait_ge(conv_sum, (TAPS_A - 1) * l + k - 4)
                            A.activation(product[:, k % 4, :], src, ACT.Copy, scale=w).then_inc(conv_mul, 1)

                for j in range(8, 12):
                    hi(sc, main, None, n0 + j, 2 * GROUPS[G_KI][1])
                    taps(4 * (j - 8), 4 * (j - 7))
                for m in range(4):
                    bank_ready(sc, l, G_QI, m)
                    A.copy(qiT[:, m, :], ps[:, 4 + m, :]).then_inc(qi_set, 1)
                bank_ready(sc, l, G_KI, 0)
                A.copy(kiT[0:64, :], ps[0:64, 0, :]).then_inc(ki_set, 1)
                A.copy(kiT[64:128, :], ps[0:64, 0, :]).then_inc(ki_set, 1)
                A.copy(wT[64:72, :], ps[64:72, 0, :]).then_inc(ki_set, 1)
                for m in range(2):
                    bank_ready(sc, l, G_KI, 1 + m)
                    A.copy(u[:, m, 16:528], ps[:, 1 + m, :]).then_inc(u_set, 1)
                sc.wait_ge(wt_ready, l + 1)
                A.activation(widx[:].rearrange("p t h -> p (t h)"), ps[:, 3, 0:TT * HEADS], ACT.Copy,
                             scale=IDX_SCALE).then_inc(widx_set, 1)
                sc.wait_ge(glu_set, 2 * (l + 1))
                for v in range(24):
                    b = v % 3 + 1
                    sc.wait_ge(dots_ready, 24 * l + v + 1)
                    if v >= 2:
                        sc.wait_ge(idx_acc, 24 * l + v - 1)
                    A.activation(lsb[:, v % 2, 0:KEYS[b]], ps[:, 4 + v % 4, 0:KEYS[b]], ACT.Relu).then_inc(relu_set, 1)
                    if 16 + v < TAPS_A:
                        taps(16 + v, 17 + v)
                    if v % 6 == 5:
                        hi(sc, main, None, n0 + 12 + v // 6)
                for j in range(16, 20):
                    hi(sc, main, None, n0 + j)
                for m in range(4):
                    bank_ready(sc, l, G_K, m)
                    A.copy(kT[:, m, :], ps[:, m, :]).then_inc(k_set, 1)
                for j in range(20, 24):
                    hi(sc, main, None, n0 + j)
                sc.wait_ge(conv_sum, (TAPS_A - 1) * (l + 1))
                for m in range(4):
                    bank_ready(sc, l, G_Q, m)
                    A.copy(qT[:, m, :], ps[:, 4 + m, :]).then_inc(q_set, 1)

                def o_hi(b):
                    sc.wait_ge(ot_ready, TT * l + b + 1)
                    A.activation(a_hi[:, 0:4, b * P:(b + 1) * P], ps[:, 2, :].rearrange("p (q n) -> p q n", q=4),
                                 ACT.Copy).then_inc(o_hi_set, 1)

                def other(s):
                    if s in OUT_SPLIT:
                        hi(sc, main, None, n0 + PIECES_IN + OUT_SPLIT.index(s))
                    if s == 7:
                        for m in range(2):
                            sc.wait_ge(ln_d, 2 * l + m + 1)
                            A.activation(sq[:, m, :], acc[:, m, :], ACT.Square).then_inc(ln_sq, 1)
                    if s == 11:
                        sc.wait_ge(ln_ms, l + 1)
                        A.activation(ln_t[:, 1, :], ln_t[:, 0, :], ACT.Sqrt).then_inc(ln_rms, 1)
                    if s == 14:
                        for m in range(2):
                            sc.wait_ge(ln_n, 2 * l + m + 1)
                            A.activation(sq[:, m, :], acc[:, m, :], ACT.Silu, scale=chan[:, l, m, V_LNG:V_LNG + 1],
                                         bias=chan[:, l, m, V_LNB:V_LNB + 1]).then_inc(ln_y, 1)
                    if s in (17, 20):
                        m = (17, 20).index(s)
                        sc.wait_ge(pw_ready, 2 * l + m + 1)
                        A.activation(a_hi[:, 6 + m, :], ps[:, 3, :], ACT.Identity,
                                     bias=chan[:, l, m, V_PWB:V_PWB + 1]).then_inc(pw_hi, 1)
                    if s in (28, 31):
                        m = (28, 31).index(s)
                        sc.wait_ge(pool_ready, 2 * l + m + 1)
                        A.activation(a_hi[:, 4 + m, :], ps[:, 3, :], ACT.Copy,
                                     scale=chan[:, l, m, V_PSC:V_PSC + 1]).then_inc(pool_hi, 1)

                for s in range(UNITS + 1):
                    if s < UNITS:
                        K = KEYS[s // HEADS]
                        sc.wait_ge(negmax_set, UNITS * l + s + 1)
                        if s >= 2:
                            sc.wait_ge(pt_ready, UNITS * l + s - 1)
                        A.activation(prob[:, s % 2, 0:K], lsb[:, s % 2, 0:K], ACT.Exp, bias=stat[:, 1, s:s + 1],
                                     scale=ATT_SCALE, accum_out=stat[:, 2, s:s + 1]).then_inc(exp_set, 1)
                    if s == 0:
                        for m in range(4):
                            bank_ready(sc, l, G_V, m)
                            A.copy(v_sb[:, m, :], ps[:, m, :]).then_inc(v_set, 1)
                    if s >= 1:
                        w = s - 1
                        K = KEYS[w // HEADS]
                        sc.wait_ge(pt_ready, UNITS * l + w + 1)
                        if w >= 2:
                            sc.wait_ge(pv_ready, UNITS * l + w - 1)
                        A.copy(pT[:, w % 2, 0:K], ps[:, 6 + w % 2, 0:K]).then_inc(pt_set, 1)
                    other(s)
                    if s >= 12 and (s - 12) % HEADS == 0:
                        o_hi((s - 12) // HEADS)
                o_hi(TT - 1)
                for j in range(4, 11):
                    hi(sc, main, None, n0 + PIECES_IN + j)
                norm_act(2 * l + 1, lambda tt: sc.wait_ge(x_mixed, 8 * l + 2 * (tt + 1)))
                hi(sc, main, None, n0 + PIECES_IN + 11)
                norm_hi(2 * l + 1)
                sc.wait_ge(rlog_ready, l + 1)
                A.copy(lgT[0:20, :], ps[0:20, 0, :]).then_inc(lgt_set, 1)
                for q in range(2):
                    sc.wait_ge(exp_in, 2 * l + q + 1)
                    A.activation((R["ge"], R["fe"])[q], (R["gd"], R["fx"])[q], ACT.Exp).then_inc(exp_out, 1)
                n = n0 + PIECES_MIX
                te, tx = E * l, (E + 1) * l
                tile_xt(main, None, tx)
                for k in range(4, 8):
                    hi(sc, main, None, n + k)
                tile_silu(main, None, n)
                tile_xt(main, None, tx + 1)
                for k in range(8, 12):
                    hi(sc, main, None, n + k)
                tile_at(main, None, te)
                n += 8

                def step(i, e):
                    m = n + e * PIECES_E
                    for k in range(4, 12):
                        hi(sc, main, i, m + k)
                    tile_silu(main, i, m)
                    tile_xt(main, i, tx + e + 2)
                    for k in range(12, 16):
                        hi(sc, main, i, m + k)
                    tile_at(main, i, te + e + 1)
                    tile_y(main, l, i, e, m + 8)

                for e in range(3):
                    step(None, e)
                with sc.Fori(2, E // 2) as i:
                    step(i, -1)
                    step(i, 0)
                tile_y(main, l, None, E - 1, n + PIECES_E * (E - 1))
                sc.wait_ge(ovx_set, l + 1)
                extra = sc.value_load(ovx[0:1, EXTRA:EXTRA + 1], min_val=0, max_val=EXTRA)
                with sc.If(extra > 0):
                    sc.wait_ge(main.w_used, (l + 1) * PIECES_L)
                    all_stored(sc, l)
                    for j in range(EXTRA):
                        O = over[l]
                        tile_xt(O, None, j)
                        for k in range(8):
                            hi(sc, O, None, PIECES_E * j + k)
                        tile_silu(O, None, PIECES_E * j)
                        tile_at(O, None, j)
                        for k in range(8, 12):
                            hi(sc, O, None, PIECES_E * j + k)
                        tile_y(O, l, None, j, PIECES_E * j + 8)
                    sc.wait_ge(over[l].w_used, EXTRA * PIECES_E)
            norm_act(2 * DEPTH, lambda tt: sc.wait_ge(x_moe, 2 * TT * (DEPTH - 1) + 2 * (tt + 1)))

        @block.vector
        def _(ve):
            V = nc.vector
            steps = [0]

            def link(ins):
                steps[0] += 1
                ins.then_inc(dve_step, 1)
                ve.wait_ge(dve_step, steps[0])

            def norm_rows(k, make=lambda tt: None):
                for tt in range(TT + 2):
                    if tt < TT:
                        make(tt)
                    if 1 <= tt <= TT:
                        ve.wait_ge(ssq_set, TT * k + tt)
                        V.tensor_scalar(nrm[:, 1, tt - 1:tt], nrm[:, 0, tt - 1:tt], 1.0 / D, EPS, ALU.mult, ALU.add).then_inc(ms_set, 1)
                    if tt >= 2:
                        w = tt - 2
                        ve.wait_ge(rms_set, TT * k + w + 1)
                        link(V.reciprocal(nrm[:, 3, w:w + 1], nrm[:, 2, w:w + 1]))
                        if w == 0:
                            ve.wait_ge(gain_in, 16 * (k + 1))
                        V.scalar_tensor_tensor(out=hrow[:, w, :], in0=x[:, w, :], scalar=nrm[:, 3, w:w + 1], in1=gain[:],
                                               op0=ALU.mult, op1=ALU.mult).then_inc(hrow_set, 1)

            def add_mixed(l, tt):
                for h in range(2):
                    if 2 * tt + h < 7:
                        ve.wait_ge(out_ready, 7 * l + 2 * tt + h + 1)
                    else:
                        ve.wait_ge(w_used, l * PIECES_L + PIECES_MIX)
                    xs = x[:, tt, h * 512:(h + 1) * 512]
                    V.tensor_tensor(xs, ps[:, 2 * tt + h, :], xs, ALU.add).then_inc(x_mixed, 1)
                ve.wait_ge(x_mixed, 8 * l + 2 * (tt + 1))

            def add_experts(l, tt):
                for k in range(TOPE):
                    ve.wait_ge(yc_in[TOPE * tt + k], 16 * (l + 1))
                    if k:
                        ve.wait_ge(x_moe, 2 * TT * l + 2 * tt + 1)
                    V.scalar_tensor_tensor(out=x[:, tt, :], in0=yc[TOPE * tt + k], scalar=gates[:, k, tt:tt + 1],
                                           in1=x[:, tt, :], op0=ALU.mult, op1=ALU.add).then_inc(x_moe, 1)
                ve.wait_ge(x_moe, 2 * TT * l + 2 * (tt + 1))

            def norm_lo(k):
                for c in range(DC):
                    ve.wait_ge(ht_hi, DC * k + c + 1)
                    V.tensor_tensor(a_lo[:, c, :], ps[:, c, :], a_hi[:, c, :].bitcast(F32), ALU.subtract).then_inc(ht_lo, 1)

            def topk_round(l, r):
                for b in range(1, TT):
                    s = 6 * r + b - 1
                    if s >= 3:
                        ve.wait_ge(topk_step, 99 * l + s - 2)
                    V.max(top8[:, b - 1, :], mask[b]).then_inc(topk_step, 1)
                for b in range(1, TT):
                    ve.wait_ge(topk_step, 99 * l + 6 * r + 3 + b - 1 - 2)
                    V.match_replace(mask[b], top8[:, b - 1, :], mask[b], NEG_TAKEN).then_inc(topk_step, 1)

            def conv(l, q):
                m, k = (1, q) if q < TAPS else (0, q - TAPS + TAPS_A)
                src, w = hpad[:, m, k:k + SEQ], chan[:, l, m, k:k + 1]
                if q == 0:
                    ve.wait_ge(y_zero, 16 * EXTRA)
                    V.tensor_scalar(acc[:, 1, :], src, w, chan[:, l, 1, V_DWB:V_DWB + 1], ALU.mult, ALU.add
                                    ).then_inc(conv_tap, 1)
                else:
                    if q == TAPS:
                        ve.wait_ge(conv_sum, (TAPS_A - 1) * (l + 1))
                    ve.wait_ge(conv_tap, TAPS_V * l + q)
                    V.scalar_tensor_tensor(out=acc[:, m, :], in0=src, scalar=w, in1=acc[:, m, :],
                                           op0=ALU.mult, op1=ALU.add).then_inc(conv_tap, 1)

            def pooling(l, part):
                table = cst[:, C_PH:C_PH + 32].rearrange("p (m n) -> p m n", m=2)
                if part == 0:
                    ve.wait_ge(u_set, 2 * (l + 1))
                    link(V.tensor_tensor(ut[:, :, 16:528], u[:, :, 16:528], u[:, :, 15:527], ALU.add))
                if part == 1:
                    link(V.tensor_tensor(pl, ut[:, :, 16:528], ut[:, :, 14:526], ALU.add))
                if part == 2:
                    V.tensor_copy(ut[:, 1, 16:20], pl[:, 1, 0:4])
                    link(V.tensor_tensor(ut[:, 1, 20:528], pl[:, 1, 4:512], pl[:, 1, 0:508], ALU.add))
                if part == 3:
                    link(V.tensor_tensor(pl[64:128, 1, :], ut[64:128, 1, 16:528], ut[64:128, 1, 8:520], ALU.add))
                    V.tensor_tensor(head[0:64], ut[0:64, :, 16:32], table[0:64], ALU.mult)
                    link(V.tensor_tensor(head[64:128], pl[64:128, :, 0:16], table[64:128], ALU.mult))
                if part in (4, 5):
                    m = part - 4
                    for r, s in ((slice(0, 64), ut[0:64, m, 16:528]), (slice(64, 128), pl[64:128, m, :])):
                        ins = V.scalar_tensor_tensor(out=ut[r, m, 16:528], in0=s, scalar=cst[r, C_PW + m:C_PW + m + 1],
                                                     in1=u[r, m, 16:528], op0=ALU.mult, op1=ALU.subtract)
                    link(ins)
                if part == 6:
                    V.tensor_tensor(ut[:, :, 16:32], head, u[:, :, 16:32], ALU.subtract).then_inc(pool_d, 1)

            def route(l):
                def b4(a):
                    return a.unsqueeze(2).to_broadcast([P, TT, 4])

                rev = cst[:, C_REV:C_REV + 4].unsqueeze(1).to_broadcast([P, TT, 4])
                by_expert = [P, TOPE, TT, E]
                V.memset(R["ms"][:, TT * E:], 0.0)
                ve.wait_ge(rtok_ready, l + 1)
                link(V.tensor_tensor(R["lg"], ps[:, 1, 0:P].rearrange("p (t n) -> p t n", t=TT)[:, :, 0:20],
                                     rb[:, l, :].unsqueeze(1).to_broadcast([P, TT, 20]), ALU.add))

                def first_of_largest(d, hot):
                    link(V.scalar_tensor_tensor(out=R["t4"], in0=d, scalar=0.0, in1=rev, op0=ALU.is_ge, op1=ALU.mult))
                    link(V.tensor_reduce(R["t1"], R["t4"], AX, ALU.max))
                    return V.tensor_tensor(hot, rev, b4(R["t1"]), ALU.is_equal)

                link(V.tensor_reduce(R["mx"], R["lg"][:, :, 0:NG], AX, ALU.max))
                V.tensor_tensor(R["gd"], R["lg"][:, :, 0:NG], b4(R["mx"]), ALU.subtract).then_inc(exp_in, 1)
                ve.wait_ge(exp_in, 2 * l + 1)
                link(first_of_largest(R["gd"], R["og"]))
                og4 = R["og"].unsqueeze(3).to_broadcast([P, TT, NG, NE])
                link(V.tensor_tensor(R["pr"], R["lg"][:, :, NG:20].rearrange("p t (g i) -> p t g i", g=NG), og4, ALU.mult))
                link(V.tensor_reduce(R["ei"], R["pr"].rearrange("p t g i -> p t i g"), AX, ALU.add))
                link(V.tensor_reduce(R["mx"], R["ei"], AX, ALU.max))
                link(V.tensor_tensor(R["fd"], R["ei"], b4(R["mx"]), ALU.subtract))
                link(first_of_largest(R["fd"], R["o1"]))
                link(V.scalar_tensor_tensor(out=R["f2"], in0=R["o1"], scalar=NEG_INADM, in1=R["fd"], op0=ALU.mult, op1=ALU.add))
                V.tensor_reduce(R["fx"], R["f2"], AX, ALU.max).then_inc(exp_in, 1)
                ve.wait_ge(exp_in, 2 * l + 2)
                link(V.tensor_tensor(R["f2"], R["f2"], b4(R["fx"]), ALU.subtract))
                link(first_of_largest(R["f2"], R["o2"]))
                for k, o in enumerate((R["o1"], R["o2"])):
                    ins = V.tensor_tensor(R["m12"][:, k].rearrange("p t (g i) -> p t g i", g=NG), og4,
                                          o.unsqueeze(2).to_broadcast([P, TT, NG, NE]), ALU.mult)
                link(ins)
                V.tensor_tensor(R["ms"][:, 0:TT * E].rearrange("p (t e) -> p t e", t=TT), R["m12"][:, 0], R["m12"][:, 1],
                                ALU.add).then_inc(route_set, 1)

                link(V.tensor_tensor(R["tm"], cst[:, C_IOTA:C_IOTA + E].unsqueeze(1).unsqueeze(1).to_broadcast(by_expert),
                                     R["m12"], ALU.mult))
                link(V.tensor_reduce(R["e2"], R["tm"], AX, ALU.add))
                V.tensor_scalar(R["d2"], R["e2"], float(1 - E), None, ALU.add)
                ve.wait_ge(exp_out, 2 * l + 2)
                link(V.tensor_reduce(R["gs"], R["ge"], AX, ALU.add))
                link(V.scalar_tensor_tensor(out=R["den"], in0=R["fe"], scalar=1.0, in1=R["gs"], op0=ALU.add, op1=ALU.mult))
                link(V.reciprocal(gates[:, 0, :], R["den"]))
                V.tensor_tensor(gates[:, 1, :], gates[:, 0, :], R["fe"], ALU.mult)

                ve.wait_ge(pos_ready, l + 1)
                here = ps[:, 2, 0:TT * E].rearrange("p (t e) -> p t e", t=TT).unsqueeze(1).to_broadcast(by_expert)
                count = ps[:, 2, TT * E:(TT + 1) * E]
                V.tensor_tensor(R["tm"], here, R["m12"], ALU.mult)
                link(V.tensor_scalar(R["ex"], count, 128.0, None, ALU.is_gt))
                for q in (256.0, 384.0):
                    link(V.scalar_tensor_tensor(out=R["ex"], in0=count, scalar=q, in1=R["ex"], op0=ALU.is_gt, op1=ALU.add))
                V.tensor_reduce(R["p2"], R["tm"], AX, ALU.add)
                link(V.tensor_tensor_scan(R["cum"], cst[:, C_ONE:C_ONE + E], R["ex"], 0.0, ALU.mult, ALU.add))
                V.tensor_scalar(R["v2"], R["p2"], 128.0, None, ALU.is_ge)
                V.tensor_scalar(R["k2"], R["p2"], 256.0, None, ALU.is_ge)
                link(V.tensor_tensor(R["base"], R["cum"], R["ex"], ALU.subtract))
                V.scalar_tensor_tensor(out=R["k2"], in0=R["p2"], scalar=384.0, in1=R["k2"], op0=ALU.is_ge, op1=ALU.add)
                link(V.tensor_tensor(R["tb"], R["base"].unsqueeze(1).unsqueeze(1).to_broadcast(by_expert), R["m12"], ALU.mult))
                V.tensor_tensor(R["c2"], R["k2"], R["v2"], ALU.add)
                link(V.tensor_reduce(R["b2"], R["tb"], AX, ALU.add))
                V.scalar_tensor_tensor(out=R["p2"], in0=R["c2"], scalar=-128.0, in1=R["p2"], op0=ALU.mult, op1=ALU.add)
                link(V.tensor_tensor(R["b2"], R["b2"], R["c2"], ALU.add))
                link(V.tensor_tensor(R["b2"], R["b2"], R["d2"], ALU.subtract))
                link(V.tensor_tensor(R["b2"], R["b2"], R["v2"], ALU.mult))
                link(V.tensor_tensor(R["e2"], R["e2"], R["b2"], ALU.add))
                for k in range(TOPE):
                    for tt in range(TT):
                        q = TT * k + tt
                        V.tensor_scalar(slot_hot[:, q, :], cst[:, C_IOTA:C_IOTA + P], R["p2"][:, k, tt:tt + 1], None, ALU.is_equal)
                        V.scalar_tensor_tensor(out=R["hot"][:, q, :], in0=cst[:, C_IOTA:C_IOTA + TILES],
                                               scalar=R["e2"][:, k, tt:tt + 1],
                                               in1=cst[:, C_TOK + tt:C_TOK + tt + 1].to_broadcast([P, TILES]),
                                               op0=ALU.is_equal, op1=ALU.mult).then_inc(hot_set, 1)
                for k in range(TOPE):
                    V.scalar_tensor_tensor(out=yidx[:].rearrange("p (t k) -> p k t", k=TOPE)[:, k, :], in0=R["e2"][:, k, :],
                                           scalar=float(P), in1=R["p2"][:, k, :], op0=ALU.mult, op1=ALU.add)
                ve.wait_ge(tab_ready, l + 1)
                V.tensor_copy(tab[:], ps[:, 3, 0:TILES]).then_inc(tab_set, 1)
                V.tensor_copy(ovx[:, EXTRA:EXTRA + 1], R["cum"][:, E - 1:E])
                link(V.tensor_tensor(R["cmp"], R["cum"].unsqueeze(1).to_broadcast([P, EXTRA, E]),
                                     cst[:, C_IOTA:C_IOTA + EXTRA].unsqueeze(2).to_broadcast([P, EXTRA, E]), ALU.is_le))
                link(V.tensor_reduce(R["oe"], R["cmp"], AX, ALU.add))
                V.tensor_scalar(ovx[:, 0:EXTRA], R["oe"], float(E - 1), None, ALU.min).then_inc(ovx_set, 1)

            def tile_xt(S, i, c):
                for h in range(2):
                    ve.wait_ge(S.xt_hi, cnt(i, 4, 2 * c + h + 1))
                    V.tensor_tensor(a_lo[:, 4 * h:4 * h + 4, 0:P], ps[:, 2 + h, :].rearrange("p (q n) -> p q n", q=4),
                                    a_hi[:, 4 * h:4 * h + 4, 0:P].bitcast(F32), ALU.subtract).then_inc(S.xt_lo, 1)

            def tile_mul(S, i, c):
                ve.wait_ge(S.silu_set, cnt(i, 2, c + 1))
                V.tensor_tensor(act, ps[:, 1, :], slu, ALU.mult).then_inc(S.act_set, 1)

            def tile_at(S, i, c):
                ve.wait_ge(S.at_hi, cnt(i, 2, c + 1))
                V.tensor_tensor(a_lo[:, 0:4, P:2 * P], ps[:, 4, :].rearrange("p (q n) -> p q n", q=4),
                                a_hi[:, 0:4, P:2 * P].bitcast(F32), ALU.subtract).then_inc(S.at_lo, 1)

            def tile_y(S, l, i, e, n):
                ve.wait_ge(S.w_used, cnt(i, RING_E, n + 4))
                rows, there, free = y_of(S, l, i, e)
                if i is not None or free:
                    ve.wait_ge(there, free)
                V.tensor_copy(rows[1], ps[:, 6, :]).then_inc(S.y_set_v, 1)

            for l in range(DEPTH):
                n0 = l * PIECES_L
                if l:
                    for j in range(4):
                        lo(ve, main, None, n0 + j)
                norm_rows(2 * l, (lambda tt: add_experts(l - 1, tt)) if l else (lambda tt: None))
                if l == 0:
                    for j in range(2):
                        lo(ve, main, None, n0 + j)
                norm_lo(2 * l)
                if l == 0:
                    for j in range(2, 4):
                        lo(ve, main, None, n0 + j)
                for j in range(4, 8):
                    lo(ve, main, None, n0 + j)
                if l == 0:
                    ve.wait_ge(chan_t, 1)
                    V.tensor_copy(chan[:].rearrange("p l h v -> p (l h v)"), ps[:, 4, 0:4 * VECS]).then_inc(chan_set, 1)
                    ve.wait_ge(pads, 8)
                for m in range(2):
                    ve.wait_ge(sig_set, 2 * l + m + 1)
                    V.tensor_tensor(hpad[:, m, 30:542], ps[:, m, :], lsb[:, m, :], ALU.mult).then_inc(glu_set, 1)
                ve.wait_ge(glu_set, 2 * (l + 1))
                if l == 0:
                    ve.wait_ge(chan_set, 1)
                    ve.wait_ge(rout_in, 16 * (2 + 2 * DEPTH))
                    link(V.tensor_copy(rw_hi[:], rw[:]))
                    V.tensor_tensor(rw_lo[:], rw[:], rw_hi[:].bitcast(F32), ALU.subtract).then_inc(rw_split, 1)
                tap = 0
                for j in range(8, 12):
                    for k in range(7):
                        conv(l, tap)
                        tap += 1
                    lo(ve, main, None, n0 + j, 2 * GROUPS[G_KI][1])
                while tap < TAPS:
                    conv(l, tap)
                    tap += 1
                ve.wait_ge(widx_set, l + 1)
                for v in range(24):
                    h, b = v // 3, v % 3 + 1
                    ve.wait_ge(relu_set, 24 * l + v + 1)
                    src, w = lsb[:, v % 2, 0:KEYS[b]], widx[:, b, h:h + 1]
                    if h == 0:
                        V.tensor_scalar(mask[b], src, w, None, ALU.mult).then_inc(idx_acc, 1)
                    else:
                        ve.wait_ge(idx_acc, 24 * l + v - 2)
                        V.scalar_tensor_tensor(out=mask[b], in0=src, scalar=w, in1=mask[b],
                                               op0=ALU.mult, op1=ALU.add).then_inc(idx_acc, 1)
                    if v % 6 == 5:
                        lo(ve, main, None, n0 + 12 + v // 6)
                    if v >= 18 and v % 1 == 0 and tap < TAPS_V:
                        conv(l, tap)
                        tap += 1
                ve.wait_ge(idx_acc, 24 * (l + 1))
                for b in range(1, TT):
                    V.memset(mask[b][0:CHUNK, KEYS[b] - CHUNK:KEYS[b]], NEG_INADM).then_inc(inadm_set, 1)
                ve.wait_ge(inadm_set, 3 * (l + 1))
                for r in range(ROUNDS):
                    if r < 12 and r % 3 != 2:
                        lo(ve, main, None, n0 + 16 + r // 3 * 2 + r % 3)
                    topk_round(l, r)
                for b in range(1, TT):
                    ve.wait_ge(topk_step, 99 * l + 96 - 2 + b - 1)
                    V.tensor_scalar(mask[b], mask[b], NEG_TEST, MASKED, ALU.is_gt, ALU.mult).then_inc(topk_step, 1)

                def o_lo(b):
                    ve.wait_ge(o_hi_set, TT * l + b + 1)
                    V.tensor_tensor(a_lo[:, 0:4, b * P:(b + 1) * P], ps[:, 2, :].rearrange("p (q n) -> p q n", q=4),
                                    a_hi[:, 0:4, b * P:(b + 1) * P].bitcast(F32), ALU.subtract).then_inc(o_lo_set, 1)

                def o_rows(b):
                    ve.wait_ge(pv_ready, UNITS * l + 8 * b + 8)
                    link(V.reciprocal(rinv[:], stat[:, 2, 8 * b:8 * b + 8]))
                    if b:
                        ve.wait_ge(ot_ready, TT * l + b)
                    V.tensor_tensor(osb.rearrange("p (h d) -> p h d", h=HEADS), ps[:, b % 2, :].rearrange("p (h d) -> p h d", h=HEADS),
                                    rinv[:].unsqueeze(2).to_broadcast([P, HEADS, HD]), ALU.mult).then_inc(o_set, 1)

                def other(s):
                    if s in OUT_SPLIT:
                        lo(ve, main, None, n0 + PIECES_IN + OUT_SPLIT.index(s))
                    if s == 6:
                        ve.wait_ge(mean_ready, l + 1)
                        for m in range(2):
                            V.scalar_tensor_tensor(out=acc[:, m, :], in0=ps[:, 3, :], scalar=-1.0 / CW, in1=acc[:, m, :],
                                                   op0=ALU.mult, op1=ALU.add).then_inc(ln_d, 1)
                    if s == 10:
                        ve.wait_ge(var_ready, l + 1)
                        V.tensor_scalar(ln_t[:, 0, :], ps[:, 3, :], 1.0 / CW, EPS, ALU.mult, ALU.add).then_inc(ln_ms, 1)
                    if s == 12:
                        ve.wait_ge(ln_rms, l + 1)
                        V.reciprocal(ln_t[:, 0, 0:256], ln_t[:, 1, 0:256])
                    if s == 13:
                        link(V.reciprocal(ln_t[:, 0, 256:512], ln_t[:, 1, 256:512]))
                        for m in range(2):
                            V.tensor_tensor(acc[:, m, :], acc[:, m, :], ln_t[:, 0, :], ALU.mult).then_inc(ln_n, 1)
                    if s in (18, 21):
                        m = (18, 21).index(s)
                        ve.wait_ge(pw_hi, 2 * l + m + 1)
                        V.scalar_tensor_tensor(out=a_lo[:, 6 + m, :], in0=ps[:, 3, :], scalar=chan[:, l, m, V_PWB:V_PWB + 1],
                                               in1=a_hi[:, 6 + m, :].bitcast(F32), op0=ALU.add, op1=ALU.subtract).then_inc(pw_lo, 1)
                    if s in (29, 32):
                        m = (29, 32).index(s)
                        ve.wait_ge(pool_hi, 2 * l + m + 1)
                        V.scalar_tensor_tensor(out=a_lo[:, 4 + m, :], in0=ps[:, 3, :], scalar=chan[:, l, m, V_PSC:V_PSC + 1],
                                               in1=a_hi[:, 4 + m, :].bitcast(F32), op0=ALU.mult, op1=ALU.subtract).then_inc(pool_lo, 1)

                for s in range(UNITS):
                    b = s // HEADS
                    if s == HEADS:
                        ve.wait_ge(topk_step, 99 * (l + 1))
                    ve.wait_ge(qk_ready, UNITS * l + s + 1)
                    if s >= 2:
                        ve.wait_ge(exp_set, UNITS * l + s - 1)
                    V.tensor_tensor_reduce(lsb[:, s % 2, 0:KEYS[b]], ps[:, 4 + s % 2, 0:KEYS[b]], mask[b], 1.0, -3.0e38,
                                           ALU.add, ALU.max, stat[:, 0, s:s + 1]).then_inc(logit_set, 1)
                    ve.wait_ge(logit_set, UNITS * l + s + 1)
                    V.tensor_scalar(stat[:, 1, s:s + 1], stat[:, 0, s:s + 1], -ATT_SCALE, None, ALU.mult).then_inc(negmax_set, 1)
                    while 1 <= s and tap < TAPS_V:
                        conv(l, tap)
                        tap += 1
                        if (tap - TAPS) % 3 == 0:
                            break
                    if s >= 10 and (s - 10) % HEADS == 0:
                        o_rows((s - 10) // HEADS)
                    if s >= 13 and (s - 13) % HEADS == 0:
                        o_lo((s - 13) // HEADS)
                    other(s)
                    if 15 <= s < 25 and s not in (18, 21):
                        pooling(l, s - 15 - (s > 18) - (s > 21))
                o_rows(TT - 1)
                other(UNITS)
                o_lo(TT - 1)
                for j in range(4, 11):
                    lo(ve, main, None, n0 + PIECES_IN + j)
                norm_rows(2 * l + 1, lambda tt: add_mixed(l, tt))
                norm_lo(2 * l + 1)
                lo(ve, main, None, n0 + PIECES_IN + 11)
                route(l)
                n = n0 + PIECES_MIX
                te, tx = E * l, (E + 1) * l
                tile_xt(main, None, tx)
                for k in range(4, 8):
                    lo(ve, main, None, n + k)
                tile_mul(main, None, te)
                tile_xt(main, None, tx + 1)
                for k in range(8, 12):
                    lo(ve, main, None, n + k)
                tile_at(main, None, te)
                n += 8

                def step(i, e):
                    m = n + e * PIECES_E
                    for k in range(4, 12):
                        lo(ve, main, i, m + k)
                    tile_mul(main, i, te + e + 1)
                    tile_xt(main, i, tx + e + 2)
                    for k in range(12, 16):
                        lo(ve, main, i, m + k)
                    tile_at(main, i, te + e + 1)
                    tile_y(main, l, i, e, m + 8)

                for e in range(3):
                    step(None, e)
                with ve.Fori(2, E // 2) as i:
                    step(i, -1)
                    step(i, 0)
                tile_y(main, l, None, E - 1, n + PIECES_E * (E - 1))
                ve.wait_ge(ovx_set, l + 1)
                extra = ve.value_load(ovx[0:1, EXTRA:EXTRA + 1], min_val=0, max_val=EXTRA)
                with ve.If(extra > 0):
                    ve.wait_ge(main.w_used, (l + 1) * PIECES_L)
                    all_stored(ve, l)
                    for j in range(EXTRA):
                        O = over[l]
                        tile_xt(O, None, j)
                        for k in range(8):
                            lo(ve, O, None, PIECES_E * j + k)
                        tile_mul(O, None, j)
                        tile_at(O, None, j)
                        for k in range(8, 12):
                            lo(ve, O, None, PIECES_E * j + k)
                        tile_y(O, l, None, j, PIECES_E * j + 8)
            norm_rows(2 * DEPTH, lambda tt: add_experts(DEPTH - 1, tt))


_INS = ["x", "norm1_g", "w_in", "pool_w", "pool_scale", "dw_w", "dw_b", "conv_ln_g", "conv_ln_b", "pw_w", "pw_b",
        "w_out", "norm2_g", "rg_w", "rg_b", "re_w", "re_b", "w_gate", "w_up", "w_down", "final_g"]


def shape_constants():
    c = np.zeros((P, C_N), np.float32)
    c[:, C_ID:C_ID + P] = np.eye(P)
    c[:, C_TRI:C_TRI + P] = np.triu(np.ones((P, P)), 1)
    c[:, C_ONE:C_ONE + P] = 1.0
    c[:, C_IOTA:C_IOTA + P] = np.arange(P)
    c[:, C_REV:C_REV + 4] = [4, 3, 2, 1]
    c[:, C_TOK:C_TOK + TT] = np.arange(SEQ).reshape(TT, P).T
    for m, r, w in ((0, 0, 2), (0, 1, 4), (1, 0, 8), (1, 1, 16)):
        rows = slice(64 * r, 64 * r + 64)
        c[rows, C_PW + m] = 1.0 / w
        c[rows, C_PH + 16 * m:C_PH + 16 * m + 16] = 1.0 / np.minimum(np.arange(1, 17), w)
    return c


def kernel(**inputs):
    import concourse.bacc as _bacc
    from concourse.bass_utils import run_bass_kernel_spmd as _run

    nc = _bacc.Bacc("TRN2", target_bir_lowering=False, num_devices=1)
    arrays, t = {}, {}
    for name in _INS + ["shape_constants"]:
        a = np.ascontiguousarray(shape_constants() if name == "shape_constants" else inputs[name])
        arrays[f"in_{name}"] = a
        t[name] = nc.dram_tensor(f"in_{name}", a.shape, mybir.dt.from_np(a.dtype), kind="ExternalInput").ap()
    for name in ("w_gate", "w_up", "w_down"):
        t[name] = t[name].rearrange("l g e a b -> (l g e) a b")
    out = nc.dram_tensor("out_0", (1, SEQ, D), F32, kind="ExternalOutput").ap()
    trunk(nc, t, out)
    r = _run(nc, [arrays], core_ids=[0])
    return r.results[0]["out_0"]
```
